# Optimizing a Trainium2 kernel written in Bass

```python
import jax, jax.numpy as jnp
from jax import lax
import numpy as np
import math

D_MODEL = 1024
BATCH = 1
SEQ = 512
DEPTH = 2

MIX_WIDTH = D_MODEL
CONV_WIDTH = MIX_WIDTH // 2
ATT_WIDTH = MIX_WIDTH - CONV_WIDTH
HEAD_DIM = 64
N_ATT_HEADS = ATT_WIDTH // HEAD_DIM
N_CONV_GROUPS = CONV_WIDTH // HEAD_DIM
CONV_K = 3
N_MEM = 256
N_XHEADS = 4
XHEAD_DIM = D_MODEL // N_XHEADS
D_FF = 2816
Q_BLOCK = 128
EPS = 1e-6
IN_COLS = 3 * CONV_WIDTH + 3 * ATT_WIDTH + N_ATT_HEADS
SPLITS = [CONV_WIDTH, 2 * CONV_WIDTH, 3 * CONV_WIDTH,
          3 * CONV_WIDTH + ATT_WIDTH, 3 * CONV_WIDTH + 2 * ATT_WIDTH,
          3 * CONV_WIDTH + 3 * ATT_WIDTH]


def rmsnorm(x, g):
    xf = x.astype(jnp.float32)
    y = xf * lax.rsqrt(jnp.mean(xf * xf, axis=-1, keepdims=True) + EPS)
    return (y * g.astype(jnp.float32)).astype(x.dtype)

def swiglu(h, w_gu, w_down):
    gate, up = jnp.split(h @ w_gu, 2, axis=-1)
    return (jax.nn.silu(gate) * up) @ w_down

def causal_depthwise_conv(u, w):
    kern = w[:, None, :].astype(u.dtype)
    return lax.conv_general_dilated(
        u, kern, window_strides=(1,), padding=[(CONV_K - 1, 0)],
        dimension_numbers=('NWC', 'WIO', 'NWC'), feature_group_count=u.shape[-1])

def forgetting_attention(q, k, v, log_f):
    B, S, H, Dh = q.shape
    nb = S // Q_BLOCK
    scale = Dh ** -0.5
    c = jnp.cumsum(log_f, axis=1).transpose(0, 2, 1)
    qb = q.reshape(B, nb, Q_BLOCK, H, Dh).transpose(1, 0, 3, 2, 4)
    cqb = c.reshape(B, H, nb, Q_BLOCK).transpose(2, 0, 1, 3)
    kpos = jnp.arange(S)

    def block(args):
        i, q_i, cq_i = args
        s = jnp.einsum('bhqd,bkhd->bhqk', q_i, k,
                       preferred_element_type=jnp.float32) * scale
        s = s + cq_i[..., None] - c[:, :, None, :]
        qpos = i * Q_BLOCK + jnp.arange(Q_BLOCK)
        mask = kpos[None, :] <= qpos[:, None]
        s = jnp.where(mask, s, -jnp.inf)
        p = jax.nn.softmax(s, axis=-1)
        return jnp.einsum('bhqk,bkhd->bqhd', p.astype(v.dtype), v)

    out = lax.map(block, (jnp.arange(nb), qb, cqb))
    return out.transpose(1, 0, 2, 3, 4).reshape(B, S, H * Dh)

def memory_cross_attention(h, m, w_q, w_kv, w_o):
    B, S, _ = h.shape
    M = m.shape[1]
    q = (h @ w_q).reshape(B, S, N_XHEADS, XHEAD_DIM)
    k, v = jnp.split(m @ w_kv, 2, axis=-1)
    k = k.reshape(B, M, N_XHEADS, XHEAD_DIM)
    v = v.reshape(B, M, N_XHEADS, XHEAD_DIM)
    s = jnp.einsum('bshd,bmhd->bhsm', q, k,
                   preferred_element_type=jnp.float32) * (XHEAD_DIM ** -0.5)
    p = jax.nn.softmax(s, axis=-1)
    o = jnp.einsum('bhsm,bmhd->bshd', p.astype(v.dtype), v).reshape(B, S, D_MODEL)
    return o @ w_o

def first_inputs(seed: int = 0) -> dict:
    key = jax.random.key(seed)
    ks = jax.random.split(key, 24)
    f32 = jnp.float32

    def w(k, shape, fan_in):
        return jax.random.normal(k, shape, f32) * (fan_in ** -0.5)

    def gain(k, shape):
        return 1.0 + 0.1 * jax.random.normal(k, shape, f32)

    return {
        "x": jax.random.normal(ks[0], (BATCH, SEQ, D_MODEL), f32),
        "mem": jax.random.normal(ks[1], (BATCH, N_MEM, D_MODEL), f32),
        "g_ffn1": gain(ks[2], (DEPTH, D_MODEL)),
        "w_ffn1_gu": w(ks[3], (DEPTH, D_MODEL, 2 * D_FF), D_MODEL),
        "w_ffn1_down": w(ks[4], (DEPTH, D_FF, D_MODEL), D_FF),
        "g_mix": gain(ks[5], (DEPTH, D_MODEL)),
        "w_mix_in": w(ks[6], (DEPTH, D_MODEL, IN_COLS), D_MODEL),
        "w_conv": w(ks[7], (DEPTH, CONV_K, CONV_WIDTH), CONV_K),
        "b_f": 2.0 + 0.5 * jax.random.normal(ks[8], (DEPTH, N_ATT_HEADS), f32),
        "g_conv_out": gain(ks[9], (DEPTH, CONV_WIDTH)),
        "g_att_out": gain(ks[10], (DEPTH, ATT_WIDTH)),
        "w_mix_out": w(ks[11], (DEPTH, MIX_WIDTH, D_MODEL), MIX_WIDTH),
        "g_xattn": gain(ks[12], (DEPTH, D_MODEL)),
        "g_mem": gain(ks[13], (DEPTH, D_MODEL)),
        "w_xq": w(ks[14], (DEPTH, D_MODEL, D_MODEL), D_MODEL),
        "w_xkv": w(ks[15], (DEPTH, D_MODEL, 2 * D_MODEL), D_MODEL),
        "w_xo": w(ks[16], (DEPTH, D_MODEL, D_MODEL), D_MODEL),
        "g_ffn2": gain(ks[17], (DEPTH, D_MODEL)),
        "w_ffn2_gu": w(ks[18], (DEPTH, D_MODEL, 2 * D_FF), D_MODEL),
        "w_ffn2_down": w(ks[19], (DEPTH, D_FF, D_MODEL), D_FF),
        "g_final": gain(ks[20], (D_MODEL,)),
    }

def first_block(x, mem, g_ffn1, w_ffn1_gu, w_ffn1_down, g_mix, w_mix_in, w_conv, b_f,
              g_conv_out, g_att_out, w_mix_out, g_xattn, g_mem, w_xq, w_xkv, w_xo,
              g_ffn2, w_ffn2_gu, w_ffn2_down, g_final):
    B, S, _ = x.shape
    for l in range(DEPTH):
        x = x + 0.5 * swiglu(rmsnorm(x, g_ffn1[l]), w_ffn1_gu[l], w_ffn1_down[l])

        h = rmsnorm(x, g_mix[l])
        z = h @ w_mix_in[l]
        zb, zc, zv, zq, zk, zval, zf = jnp.split(z, SPLITS, axis=-1)

        y_conv = zb * causal_depthwise_conv(zc * zv, w_conv[l])

        log_f = jax.nn.log_sigmoid((zf + b_f[l]).astype(jnp.float32))
        q = zq.reshape(B, S, N_ATT_HEADS, HEAD_DIM)
        k = zk.reshape(B, S, N_ATT_HEADS, HEAD_DIM)
        v = zval.reshape(B, S, N_ATT_HEADS, HEAD_DIM)
        y_att = forgetting_attention(q, k, v, log_f)

        y = jnp.concatenate([rmsnorm(y_conv, g_conv_out[l]),
                             rmsnorm(y_att, g_att_out[l])], axis=-1)
        x = x + y @ w_mix_out[l]

        x = x + memory_cross_attention(rmsnorm(x, g_xattn[l]), rmsnorm(mem, g_mem[l]),
                                       w_xq[l], w_xkv[l], w_xo[l])

        x = x + 0.5 * swiglu(rmsnorm(x, g_ffn2[l]), w_ffn2_gu[l], w_ffn2_down[l])
    return rmsnorm(x, g_final)


N_A_LAYERS = DEPTH // 2
N_B_LAYERS = DEPTH - N_A_LAYERS
QB = 128
DA_HEAD_DIM = 64
DA_HEADS = D_MODEL // (2 * DA_HEAD_DIM)
DA_QK = DA_HEADS * 2 * DA_HEAD_DIM
DA_V = DA_HEADS * 2 * DA_HEAD_DIM
DA_IN = 2 * DA_QK + DA_V + DA_V
LAMBDA_INIT = tuple(0.8 - 0.6 * math.exp(-0.3 * l) for l in range(N_A_LAYERS))
SB_HEAD_DIM = 64
SB_HEADS = D_MODEL // SB_HEAD_DIM
SB_W = SB_HEADS * SB_HEAD_DIM
SB_IN = SB_W + SB_W
ROPE_THETA = 500000.0
ROT_DIM = DA_HEAD_DIM // 4
RMS_EPS = 1e-6


def _rms(x, g):
    xf = x.astype(jnp.float32)
    y = xf * lax.rsqrt(jnp.mean(xf * xf, axis=-1, keepdims=True) + RMS_EPS)
    return (y * g.astype(jnp.float32)).astype(x.dtype)

def _rope_partial(t, pos):
    half = ROT_DIM // 2
    inv = jnp.power(jnp.float32(ROPE_THETA), -jnp.arange(half, dtype=jnp.float32) / half)
    ang = pos.astype(jnp.float32)[:, None] * inv[None, :]
    cos = jnp.cos(ang)[None, :, None, :]
    sin = jnp.sin(ang)[None, :, None, :]
    t1 = t[..., :half].astype(jnp.float32)
    t2 = t[..., half:ROT_DIM].astype(jnp.float32)
    rot = jnp.concatenate([t1 * cos - t2 * sin, t1 * sin + t2 * cos], axis=-1)
    return jnp.concatenate([rot.astype(t.dtype), t[..., ROT_DIM:]], axis=-1)

def _to_blocks(t):
    b, s, h, d = t.shape
    return t.reshape(b, s // QB, QB, h, d).transpose(1, 0, 3, 2, 4)

def _from_blocks(o):
    nb, b, h, qb, e = o.shape
    return o.transpose(1, 0, 3, 2, 4).reshape(b, nb * qb, h, e)

def _diff_attention(q1, q2, k1, k2, v, lam):
    s_len = q1.shape[1]
    kpos = jnp.arange(s_len)
    scale = DA_HEAD_DIM ** -0.5

    def block(args):
        i, qb1, qb2 = args
        qpos = i * QB + jnp.arange(QB)
        mask = kpos[None, :] <= qpos[:, None]

        def probs(qb, k):
            s = jnp.einsum('bhqd,bshd->bhqs', qb, k).astype(jnp.float32) * scale
            return jax.nn.softmax(jnp.where(mask, s, -jnp.inf), axis=-1)

        a = probs(qb1, k1) - lam * probs(qb2, k2)
        return jnp.einsum('bhqs,bshe->bhqe', a.astype(v.dtype), v)

    nb = s_len // QB
    o = lax.map(block, (jnp.arange(nb), _to_blocks(q1), _to_blocks(q2)))
    return _from_blocks(o)

def _stick_breaking(q, k, v):
    s_len = q.shape[1]
    kpos = jnp.arange(s_len)
    scale = SB_HEAD_DIM ** -0.5

    def block(args):
        i, qb = args
        qpos = i * QB + jnp.arange(QB)
        mask = kpos[None, :] < qpos[:, None]
        z = jnp.einsum('bhqd,bshd->bhqs', qb, k).astype(jnp.float32) * scale
        log_beta = jax.nn.log_sigmoid(z)
        log_1mb = jnp.where(mask, jax.nn.log_sigmoid(-z), 0.0)
        suffix = lax.cumsum(log_1mb, axis=3, reverse=True) - log_1mb
        a = jnp.where(mask, jnp.exp(log_beta + suffix), 0.0)
        return jnp.einsum('bhqs,bshe->bhqe', a.astype(v.dtype), v)

    nb = s_len // QB
    o = lax.map(block, (jnp.arange(nb), _to_blocks(q)))
    return _from_blocks(o)

def _diff_layer(x, pos, norm_g, w_in, w_out, q_norm, k_norm, lq1, lk1, lq2, lk2,
                subln, lambda_init):
    b, s, _ = x.shape
    h = _rms(x, norm_g)
    proj = h @ w_in
    q, k, v, g = jnp.split(proj, [DA_QK, 2 * DA_QK, 2 * DA_QK + DA_V], axis=-1)
    q = q.reshape(b, s, DA_HEADS, 2, DA_HEAD_DIM)
    k = k.reshape(b, s, DA_HEADS, 2, DA_HEAD_DIM)
    v = v.reshape(b, s, DA_HEADS, 2 * DA_HEAD_DIM)
    qs = [_rope_partial(_rms(q[:, :, :, c], q_norm), pos) for c in range(2)]
    ks = [_rope_partial(_rms(k[:, :, :, c], k_norm), pos) for c in range(2)]
    lam = (jnp.exp(jnp.sum(lq1.astype(jnp.float32) * lk1.astype(jnp.float32)))
           - jnp.exp(jnp.sum(lq2.astype(jnp.float32) * lk2.astype(jnp.float32)))
           + lambda_init)
    o = _diff_attention(qs[0], qs[1], ks[0], ks[1], v, lam)
    o = _rms(o, subln) * (1.0 - lambda_init)
    o = o.reshape(b, s, DA_V) * jax.nn.silu(g)
    return x + o @ w_out

def _shared_kv(x, kv_norm, w_kv):
    b, s, _ = x.shape
    kv = _rms(x, kv_norm) @ w_kv
    k, v = jnp.split(kv, [SB_W], axis=-1)
    return (k.reshape(b, s, SB_HEADS, SB_HEAD_DIM), v.reshape(b, s, SB_HEADS, SB_HEAD_DIM))

def _sb_layer(x, k, v, norm_g, w_in, w_out):
    b, s, _ = x.shape
    proj = _rms(x, norm_g) @ w_in
    q, g = jnp.split(proj, [SB_W], axis=-1)
    o = _stick_breaking(q.reshape(b, s, SB_HEADS, SB_HEAD_DIM), k, v)
    o = o.reshape(b, s, SB_W) * jax.nn.silu(g)
    return x + o @ w_out

def second_inputs(seed: int = 0) -> dict:
    key = jax.random.key(seed)
    ks = jax.random.split(key, 20)
    f32 = jnp.float32
    nrm = lambda k, shape, scale: jax.random.normal(k, shape, f32) * scale
    gain = lambda k, shape: 1.0 + 0.02 * jax.random.normal(k, shape, f32)
    return {
        "x": jax.random.normal(ks[0], (BATCH, SEQ, D_MODEL), f32),
        "a_norm": gain(ks[1], (N_A_LAYERS, D_MODEL)),
        "a_w_in": nrm(ks[2], (N_A_LAYERS, D_MODEL, DA_IN), D_MODEL ** -0.5),
        "a_w_out": nrm(ks[3], (N_A_LAYERS, DA_V, D_MODEL), DA_V ** -0.5),
        "a_q_norm": gain(ks[4], (N_A_LAYERS, DA_HEAD_DIM)),
        "a_k_norm": gain(ks[5], (N_A_LAYERS, DA_HEAD_DIM)),
        "a_lq1": nrm(ks[6], (N_A_LAYERS, DA_HEAD_DIM), 0.1),
        "a_lk1": nrm(ks[7], (N_A_LAYERS, DA_HEAD_DIM), 0.1),
        "a_lq2": nrm(ks[8], (N_A_LAYERS, DA_HEAD_DIM), 0.1),
        "a_lk2": nrm(ks[9], (N_A_LAYERS, DA_HEAD_DIM), 0.1),
        "a_subln": gain(ks[10], (N_A_LAYERS, 2 * DA_HEAD_DIM)),
        "kv_norm": gain(ks[11], (D_MODEL,)),
        "w_kv": nrm(ks[12], (D_MODEL, 2 * SB_W), D_MODEL ** -0.5),
        "b_norm": gain(ks[13], (N_B_LAYERS, D_MODEL)),
        "b_w_in": nrm(ks[14], (N_B_LAYERS, D_MODEL, SB_IN), D_MODEL ** -0.5),
        "b_w_out": nrm(ks[15], (N_B_LAYERS, SB_W, D_MODEL), SB_W ** -0.5),
    }

def second_block(x, a_norm, a_w_in, a_w_out, a_q_norm, a_k_norm, a_lq1, a_lk1, a_lq2,
              a_lk2, a_subln, kv_norm, w_kv, b_norm, b_w_in, b_w_out):
    pos = jnp.arange(x.shape[1])
    shared_k = None
    shared_v = None
    for layer in range(DEPTH):
        if layer < N_A_LAYERS:
            x = _diff_layer(x, pos, a_norm[layer], a_w_in[layer], a_w_out[layer],
                            a_q_norm[layer], a_k_norm[layer], a_lq1[layer], a_lk1[layer],
                            a_lq2[layer], a_lk2[layer], a_subln[layer], LAMBDA_INIT[layer])
        else:
            if layer == N_A_LAYERS:
                shared_k, shared_v = _shared_kv(x, kv_norm, w_kv)
            j = layer - N_A_LAYERS
            x = _sb_layer(x, shared_k, shared_v, b_norm[j], b_w_in[j], b_w_out[j])
    return x


def setup_inputs(seed=0):
    out = dict(first_inputs(seed))
    for name, value in second_inputs(seed + 1).items():
        if name != "x":
            out[name + "_2"] = value
    return out


def reference(
    x, mem, g_ffn1, w_ffn1_gu, w_ffn1_down, g_mix, w_mix_in, w_conv, b_f, g_conv_out, g_att_out,
    w_mix_out, g_xattn, g_mem, w_xq, w_xkv, w_xo, g_ffn2, w_ffn2_gu, w_ffn2_down, g_final,
    a_norm_2, a_w_in_2, a_w_out_2, a_q_norm_2, a_k_norm_2, a_lq1_2, a_lk1_2, a_lq2_2, a_lk2_2,
    a_subln_2, kv_norm_2, w_kv_2, b_norm_2, b_w_in_2, b_w_out_2,
):
    x = first_block(
        x, mem, g_ffn1, w_ffn1_gu, w_ffn1_down, g_mix, w_mix_in, w_conv, b_f, g_conv_out,
        g_att_out, w_mix_out, g_xattn, g_mem, w_xq, w_xkv, w_xo, g_ffn2, w_ffn2_gu, w_ffn2_down,
        g_final,
    )
    return second_block(
        x, a_norm_2, a_w_in_2, a_w_out_2, a_q_norm_2, a_k_norm_2, a_lq1_2, a_lk1_2, a_lq2_2,
        a_lk2_2, a_subln_2, kv_norm_2, w_kv_2, b_norm_2, b_w_in_2, b_w_out_2,
    )


_drawn_inputs = setup_inputs


def setup_inputs(seed=0):
    import zlib

    import numpy as np

    out = dict(_drawn_inputs(seed))
    spreads = {}
    factors = {'g_xattn': 4.27,
     'a_norm_2': 3.448,
     'a_q_norm_2': 8.0,
     'a_k_norm_2': 6.895,
     'a_lq1_2': 3.239,
     'a_subln_2': 5.957,
     'kv_norm_2': 7.131,
     'b_norm_2': 7.203}
    for name, (base, spread) in spreads.items():
        noise = np.random.default_rng([zlib.crc32(name.encode()), seed]).standard_normal(out[name].shape)
        drawn = base * np.exp(spread * noise) if base else spread * noise
        out[name] = __import__('jax').numpy.asarray(drawn.astype(out[name].dtype))
    for name, factor in factors.items():
        out[name] = (out[name] * factor).astype(out[name].dtype)
    return out
```

```python
from contextlib import ExitStack

import numpy as np

import concourse.bass as bass
from concourse import mybir

F32 = mybir.dt.float32
F32R = mybir.dt.float32r
ALU = mybir.AluOpType
ACT = mybir.ActivationFunctionType
AX = mybir.AxisListType.X

T = 512
D = 1024
KT = 8
FF = 2816
NF = FF // 128
CW = 512
EPS = 1e-6
BIG = -1.0e30
LAMBDA_INIT = 0.8 - 0.6 * float(np.exp(0.0))
NSLOT = 4
NRAW = 3
NS = 6
STAGES = ["ffn1_0", "mix_0", "x_0", "ffn2_0", "ffn1_1", "mix_1", "x_1", "ffn2_1", "diff", "sb"]

C_ID, C_MQ, C_MK, C_TRI, C_ROT, C_COS, C_SIN, C_BLK, C_N = 0, 128, 256, 384, 512, 640, 1152, 1664, 1666


def shape_constants():
    c = np.zeros((128, C_N), np.float32)
    a = np.arange(128)
    c[:, C_ID:C_ID + 128] = np.eye(128)
    c[:, C_MQ:C_MQ + 128] = np.where(a[None, :] > a[:, None], BIG, 0.0)
    c[:, C_MK:C_MK + 128] = np.where(a[None, :] <= a[:, None], BIG, 0.0)
    c[:, C_TRI:C_TRI + 128] = np.where(a[:, None] >= a[None, :], -1.0, 0.0)
    half = 8
    inv = np.power(np.float32(500000.0), -np.arange(half, dtype=np.float32) / np.float32(half)).astype(np.float32)
    ang = (np.arange(T, dtype=np.float32)[:, None] * inv[None, :]).astype(np.float32)
    cos, sin = np.cos(ang).T, np.sin(ang).T
    c[:, C_COS:C_COS + T] = 1.0
    for b in (0, 64):
        for j in range(half):
            c[b + j, C_COS:C_COS + T] = cos[j]
            c[b + half + j, C_COS:C_COS + T] = cos[j]
            c[b + j, C_SIN:C_SIN + T] = -sin[j]
            c[b + half + j, C_SIN:C_SIN + T] = sin[j]
            c[b + half + j, C_ROT + b + j] = 1.0
            c[b + j, C_ROT + b + half + j] = 1.0
    c[0:64, C_BLK] = 1.0
    c[64:128, C_BLK + 1] = 1.0
    return c


class Later:

    def activation(self, *a, **k):
        return lambda e: e.activation(*a, **k)

    def affine_select(self, *a, **k):
        return lambda e: e.affine_select(*a, **k)

    def dma_start(self, *a, **k):
        return lambda e: e.dma_start(*a, **k)

    def matmul(self, *a, **k):
        return lambda e: e.matmul(*a, **k)

    def memset(self, *a, **k):
        return lambda e: e.memset(*a, **k)

    def preload_act_table_set(self, *a, **k):
        return lambda e: e.preload_act_table_set(*a, **k)

    def reciprocal(self, *a, **k):
        return lambda e: e.reciprocal(*a, **k)

    def reduce_max(self, *a, **k):
        return lambda e: e.reduce_max(*a, **k)

    def reduce_sum(self, *a, **k):
        return lambda e: e.reduce_sum(*a, **k)

    def scalar_tensor_tensor(self, *a, **k):
        return lambda e: e.scalar_tensor_tensor(*a, **k)

    def tensor_copy(self, *a, **k):
        return lambda e: e.tensor_copy(*a, **k)

    def tensor_scalar(self, *a, **k):
        return lambda e: e.tensor_scalar(*a, **k)

    def tensor_tensor(self, *a, **k):
        return lambda e: e.tensor_tensor(*a, **k)

    def tensor_tensor_scan(self, *a, **k):
        return lambda e: e.tensor_tensor_scan(*a, **k)

    def transpose(self, *a, **k):
        return lambda e: e.transpose(*a, **k)


LATER = Later()


class Queues:

    def __init__(self):
        self.items = {e: [] for e in ("pe", "act", "dve", "pool", "sp")}
        self.count = {}
        self.met = {e: {} for e in self.items}

    def put(self, eng, fn, *waits, sem=None, by=1, mark=True):
        need = {}
        if eng == "pool" and self.count.get("pool"):
            waits = (waits, ("pool", self.count["pool"]))
        for w in flat(waits):
            need[w[0]] = max(need.get(w[0], 0), w[1])
        met = self.met[eng]
        ws = [(s, v) for s, v in need.items() if met.get(s, 0) < v]
        met.update(ws)
        sem = sem or eng
        if mark:
            self.count[sem] = self.count.get(sem, 0) + by
        self.items[eng].append((ws, fn and fn(LATER), (sem, by) if mark else None))
        return (sem, self.count[sem]) if mark else None

    def now(self):
        return [(e, self.count.get(e, 0)) for e in ("pe", "act", "dve", "pool")]

    def hold(self, eng, waits):
        self.put(eng, None, waits, mark=False)

    def run(self, eng, e, sems):
        for ws, fn, inc in self.items[eng]:
            for s, v in ws:
                e.wait_ge(sems[s], v)
            if fn is not None:
                ins = fn(e)
                if inc:
                    ins.then_inc(sems[inc[0]], inc[1])


def flat(w):
    if w is None:
        return
    if isinstance(w, tuple) and len(w) == 2 and isinstance(w[0], str):
        yield w
        return
    for x in w:
        yield from flat(x)


class Buf:

    def __init__(self, ap):
        self.ap = ap
        self.free = []


def program(nc, a, consts, out, stages):
    q = Queues()
    put = q.put
    ctx = ExitStack()
    with ctx:
        def sb(name, shape, dt=F32):
            return ctx.enter_context(nc.sbuf_tensor(name, shape, dt))

        X = sb("X", [128, KT, T])
        XH = sb("XH", [128, KT, T], F32R)
        XL = sb("XL", [128, KT, T], F32R)
        RAW = sb("RAW", [128, NRAW, 1024])
        WH = sb("WH", [128, NSLOT, 1024], F32R)
        WL = sb("WL", [128, NSLOT, 1024], F32R)
        AR = sb("AR", [128, 88 * 256], F32R)
        AF = sb("AF", [128, 3108])
        SC = sb("SC", [128, NS, T])
        RB = sb("RB", [128, T])
        IDR = sb("IDR", [128, 128], F32R)
        ID = IDR[:, :].bitcast(F32)
        GA = sb("GA", [128, 128])
        GB = sb("GB", [128, 32])
        SM = sb("SM", [128, 72])
        PS = [ctx.enter_context(nc.psum_tensor(f"PS{i}", [128, 512], F32)) for i in range(8)]
        bank = [Buf(p) for p in PS]
        S = [Buf(SC[:, i, :]) for i in range(NS)]

        ONE = SM[:, 0:1]
        BLK = SM[:, 1:3]
        NH = SM[:, 3:11]
        RCOL = SM[:, 11:15]
        MS = SM[:, 15:23]
        PW = SM[:, 23:31]
        MX = SM[:, 31:33]
        NB = SM[:, 33:35]
        LS = SM[:, 35:37]
        RL = SM[:, 37:39]
        MSS = SM[:, 39:43]
        GG = SM[:, 43:51]
        LAM = SM[:, 51:52]
        QG = SM[:, 52:53]
        SG = SM[:, 53:54]
        BF = SM[:, 54:56]
        LT = SM[:, 56:60]
        NL = SM[:, 60:61]

        def F(ap):
            return ap.bitcast(F32)

        names = set()

        units = []

        def plan(key, ap, gain=None, kind="w"):
            units.append((key, ap, gain, kind))

        def plan_cols(name, w, c0, cols=256, gain=None, nk=KT):
            for u in range(0, nk, 4):
                n = min(4, nk - u)
                src = w[u * 128:(u + n) * 128, c0:c0 + cols].rearrange("(k p) c -> p k c", p=128)
                plan((name, u // 4), src, None if gain is None else (gain, u))

        raws = [Buf(RAW[:, i, :]) for i in range(NRAW)]
        slots = [Buf(None) for _ in range(NSLOT)]
        state = {"dma": 0, "split": 0, "slotseq": 0}
        loaded = {}
        ready = {}
        held = [False] * NSLOT
        rawheld = [False] * NRAW

        def pump():
            while True:
                moved = False
                n = state["dma"]
                if n < len(units) and not rawheld[n % NRAW]:
                    key, ap, gain, kind = units[n]
                    r = raws[n % NRAW]
                    sh = ap.shape
                    dst = r.ap[:, 0:sh[1] * sh[2]].rearrange("p (k c) -> p k c", c=sh[2])
                    tok = put("sp", lambda e, d=dst, s=ap: e.dma_start(d, s), r.free, sem=f"raw{n % NRAW}", by=16)
                    loaded[n] = (tok, dst)
                    rawheld[n % NRAW] = True
                    state["dma"] += 1
                    moved = True
                m = state["split"]
                if m < state["dma"]:
                    key, ap, gain, kind = units[m]
                    tok, dst = loaded[m]
                    if kind == "raw":
                        ready[key] = (dst, tok, m)
                        state["split"] += 1
                        moved = True
                    elif not held[state["slotseq"] % NSLOT]:
                        s = state["slotseq"] % NSLOT
                        state["slotseq"] += 1
                        held[s] = True
                        nk, ncol = ap.shape[1], ap.shape[2]
                        pc = 128 if kind == "pad" else ncol
                        h = WH[:, s, 0:nk * pc].rearrange("p (k c) -> p k c", c=pc)
                        l = WL[:, s, 0:nk * pc].rearrange("p (k c) -> p k c", c=pc)
                        fr = slots[s].free
                        if kind == "pad":
                            z1 = put("pool", lambda e, h=h: e.memset(F(h), 0.0), fr)
                            z2 = put("pool", lambda e, l=l: e.memset(F(l), 0.0), fr)
                            fr = [z1, z2]
                        hd, ld = h[:, :, 0:ncol], l[:, :, 0:ncol]
                        if gain is None:
                            t1 = put("act", lambda e, o=hd, i=dst: e.activation(o, i, ACT.Copy), tok, fr)
                            t2 = put("dve", lambda e, o=ld, i=dst, h=hd: e.tensor_tensor(o, i, F(h), ALU.subtract), t1, fr)
                        else:
                            g0, ku = gain
                            for k in range(nk):
                                gc = GA[:, g0 + ku + k:g0 + ku + k + 1]
                                t1 = put("act", lambda e, o=hd[:, k, :], i=dst[:, k, :], g=gc: e.activation(o, i, ACT.Copy, scale=g), tok, fr)
                                t2 = put("dve", lambda e, o=ld[:, k, :], i=dst[:, k, :], h=hd[:, k, :], g=gc:
                                         e.scalar_tensor_tensor(o, i, g, F(h), ALU.mult, ALU.subtract), t1, fr)
                        raws[m % NRAW].free = [t1, t2]
                        rawheld[m % NRAW] = False
                        ready[key] = (h, l, [t1, t2], s)
                        state["split"] += 1
                        moved = True
                if not moved:
                    return

        def get(key):
            pump()
            assert key in ready, (key, units[state["split"]][0] if state["split"] < len(units) else None)
            return ready.pop(key)

        def done(u, tok):
            slots[u[3]].free = [tok]
            held[u[3]] = False

        def raw_done(u, toks):
            raws[u[2] % NRAW].free = toks
            rawheld[u[2] % NRAW] = False

        def mm(o, l, r, waits=(), start=True, stop=True, mark=True, skip=False):
            return put("pe", lambda e: e.matmul(o, l, r, start=start, stop=stop, skip_group_check=skip), waits, mark=mark)

        def mm3(o, lh, ll, rh, rl, waits, start, stop, mark=False, skip=False):
            mm(o, ll, rh, waits, start, False, False, skip)
            mm(o, lh, rl, (), False, False, False, skip)
            return mm(o, lh, rh, (), False, stop, mark, skip)

        def pe_transpose(o, i, idn, waits, mark):
            return put("pe", lambda e: e.transpose(o, i, idn), waits, mark=mark)

        xtok = [None] * KT

        def xk(k):
            return XH[:, k, :], XL[:, k, :]

        def tiles(name, banks, rhs, rtok, ks=None, toks=None, cols=2, nu=2, n=T, part=None):
            us = []
            for u in range(nu):
                w = get((name, u))
                nk = w[0].shape[1]
                for k in range(nk):
                    kk = 4 * u + k
                    rh, rl = rhs(kk)
                    last = u == nu - 1 and k == nk - 1
                    for c in range(cols):
                        b = banks[c]
                        t = mm3(b.ap[:, 0:n], w[0][:, k, c * 128:(c + 1) * 128], w[1][:, k, c * 128:(c + 1) * 128],
                                rh, rl, [w[2] if k == 0 and c == 0 else None, rtok[kk] if c == 0 else None,
                                         b.free if kk == 0 else None],
                                kk == 0, last, mark=last or (k == nk - 1 and c == cols - 1))
                        if last:
                            us.append(t)
                done(w, t)
                pump()
                yield
            toks.extend(us)

        def two_chunks(n0, n1, banks, rhs, rtok, toks):
            ws = [get((n0, 0)), None, get((n1, 0)), None]

            def part(j, ks, fin):
                ch, u = divmod(j, 2)
                w = ws[j]
                for k in ks:
                    kk = 4 * u + k
                    rh, rl = rhs(kk)
                    for c in range(2):
                        b = banks[2 * ch + c]
                        t = mm3(b.ap[:, :], w[0][:, k, c * 128:(c + 1) * 128], w[1][:, k, c * 128:(c + 1) * 128],
                                rh, rl, [w[2], rtok[kk], b.free if kk == 0 else None], kk == 0, kk == 7,
                                mark=kk == 7 or (k == ks[-1] and c == 1))
                        if kk == 7:
                            toks[2 * ch + c] = t
                if fin:
                    done(w, t)
                    pump()

            part(0, range(4), True)
            yield
            ws[1] = get((n0, 1))
            part(2, range(4), True)
            yield
            ws[3] = get((n1, 1))
            part(1, (0, 1), False)
            yield
            part(3, (0, 1), False)
            yield
            part(1, (2, 3), True)
            yield
            part(3, (2, 3), True)
            yield

        def drain(g):
            for _ in g:
                pass

        def both(main, side, per=1):
            acc = 0.0
            for _ in main:
                acc += per
                while acc >= 1:
                    acc -= 1
                    next(side, None)

        def chain(*gs):
            for g in gs:
                yield from g

        rb = Buf(RB[:, :])
        rbt = {"rb": None, "rcol": None}

        def inv_rms(bk, n, width, waits_pe, lhs, rhs, r4, r4ap, groups, mark_rcol=None, ms=MS, pw=PW):
            for i in range(4):
                t = mm(bk.ap[:, i * groups:(i + 1) * groups], lhs(i), rhs, [waits_pe, bk.free if i == 0 else None], mark=i == 3)
            m = 4 * groups
            t1 = put("dve", lambda e: e.tensor_scalar(ms[:, 0:m], bk.ap[:, 0:m], 1.0 / width, EPS, ALU.mult, ALU.add),
                     t, pwfree["ms"])
            bk.free = [t1]
            dst = mark_rcol if mark_rcol is not None else pw[:, 0:m]
            t2 = put("pool", lambda e: e.tensor_tensor(dst, ms[:, 0:m], NH[:, 0:m], ALU.pow), t1, pwfree["pw"],
                     pwfree["rcol"] if mark_rcol is not None else None)
            pwfree["ms"] = [t2]
            w = 128 // groups
            src = dst.rearrange("p (i g) -> p i g", g=groups).unsqueeze(3).to_broadcast([128, 4, groups, w])
            d4 = r4ap.rearrange("p (i g w) -> p i g w", i=4, g=groups)
            if groups == 1:
                src = dst.unsqueeze(2).to_broadcast([128, 4, 128])
                d4 = r4ap.rearrange("p (i w) -> p i w", i=4)
            t3 = put("dve", lambda e: e.tensor_copy(d4, src), t2, r4.free)
            if mark_rcol is None:
                pwfree["pw"] = [t3]
            return t2, t3

        pwfree = {"ms": [], "pw": [], "rcol": []}

        def spread(bk, r4, r4ap, tok):
            for i in range(4):
                t = pe_transpose(bk.ap[:, i * 128:(i + 1) * 128], r4ap[:, i * 128:(i + 1) * 128], ID,
                                 [tok, bk.free if i == 0 else None], i == 3)
            r4.free = [t]
            return t

        accx = {"tok": None}

        def x_norm_a():
            acc = S[5]
            r, t = inv_rms(bank[6], 1, D, accx["tok"], lambda i: acc.ap[:, i * 128:(i + 1) * 128], ONE, S[4], S[4].ap, 1,
                           mark_rcol=RCOL)
            acc.free = q.now()[:1]
            rbt["rcol"] = r
            rbt["r4"] = t

        def x_norm_b():
            t = spread(bank[6], S[4], S[4].ap, rbt["r4"])
            t2 = put("act", lambda e: e.activation(RB[:, :], bank[6].ap[:, :], ACT.Copy), t, rb.free)
            bank[6].free = [t2]
            rbt["rb"] = t2

        def barrier(snap):
            for e in ("act", "dve", "pool"):
                q.hold(e, [t for t in snap if t[0] != e])

        def x_post(m, tx, gcol):
            if gcol is None:
                th = put("act", lambda e: e.activation(XH[:, m, :], X[:, m, :], ACT.Copy), tx)
                tl = put("dve", lambda e: e.tensor_tensor(XL[:, m, :], X[:, m, :], F(XH[:, m, :]), ALU.subtract), th, tx)
            else:
                g = gcol(m)
                th = put("act", lambda e: e.activation(XH[:, m, :], X[:, m, :], ACT.Copy, scale=g), tx)
                tl = put("dve", lambda e: e.scalar_tensor_tensor(XL[:, m, :], X[:, m, :], g, F(XH[:, m, :]), ALU.mult, ALU.subtract), th, tx)
            xtok[m] = [th, tl]
            square_x(m, tx)

        def square_x(m, tx):
            acc, sq = S[5], S[4]
            if m == 0:
                accx["tok"] = put("act", lambda e: e.activation(acc.ap, X[:, m, :], ACT.Square), tx, acc.free)
            else:
                ts = put("act", lambda e: e.activation(sq.ap, X[:, m, :], ACT.Square), tx, sq.free)
                accx["tok"] = put("pool", lambda e: e.tensor_tensor(acc.ap, acc.ap, sq.ap, ALU.add), ts, accx["tok"])
                sq.free = [accx["tok"]]

        def resid(m, b, tok, scale, gcol):
            tx = put("dve", lambda e: e.scalar_tensor_tensor(X[:, m, :], b.ap[:, :], scale, X[:, m, :], ALU.mult, ALU.add), tok)
            b.free = [tx]
            x_post(m, tx, gcol)

        def gc(base):
            return lambda m: GA[:, base + m:base + m + 1]

        def plan_ffn(tag, wgu, wd):
            for c in range(NF // 2):
                plan_cols(f"{tag}g{c}", wgu, c * 256)
                plan_cols(f"{tag}u{c}", wgu, FF + c * 256)
            for p in range(4):
                plan_cols(f"{tag}d{p}", wd, p * 256, nk=NF)

        def ffn(tag, snap, gnext):
            AH = AR[:, 0:NF * T].rearrange("p (f t) -> p f t", t=T)
            AL = AR[:, NF * T:2 * NF * T].rearrange("p (f t) -> p f t", t=T)
            atok = [None] * NF

            def evac(f, g, u, tg, tu):
                s, t_, w = S[f % 2], S[2 + f % 2], Buf(AF[:, (f % 2) * T:(f % 2) * T + T])
                w.free = wfree[f % 2]
                a1 = put("dve", lambda e: e.tensor_tensor(s.ap, g.ap[:, :], RB[:, :], ALU.mult), tg, rbt["rb"], s.free)
                g.free = [a1]
                a2 = put("act", lambda e: e.activation(t_.ap, s.ap, ACT.Tanh, scale=0.5), a1, t_.free)
                a3 = put("dve", lambda e: e.tensor_tensor(w.ap, u.ap[:, :], RB[:, :], ALU.mult), tu, w.free)
                u.free = [a3]
                return s, t_, w, a1, a2, a3

            def evac2(f, st):
                s, t_, w, a1, a2, a3 = st
                a4 = put("dve", lambda e: e.tensor_tensor(w.ap, s.ap, w.ap, ALU.mult), a1, a3)
                s.free = [a4]
                return a4

            def evac3(f, st, a4):
                s, t_, w, a1, a2, a3 = st
                a5 = put("dve", lambda e: e.scalar_tensor_tensor(w.ap, t_.ap, 1.0, w.ap, ALU.add, ALU.mult), a2, a4)
                t_.free = [a5]
                return put("act", lambda e: e.activation(AH[:, f, :], w.ap, ACT.Copy), a5), a5

            def evac4(f, st, a6, a5):
                w = st[2]
                a7 = put("dve", lambda e: e.tensor_tensor(AL[:, f, :], w.ap, F(AH[:, f, :]), ALU.subtract), a5, a6)
                wfree[f % 2] = [a7]
                atok[f] = [a6, a7]

            wfree = [[], []]

            def evac_pair(c, bs, tk):
                st = [evac(2 * c + j, bs[j], bs[2 + j], tk[j], tk[2 + j]) for j in range(2)]
                yield
                r = [evac2(2 * c + j, st[j]) for j in range(2)]
                r = [evac3(2 * c + j, st[j], r[j]) for j in range(2)]
                yield
                for j in range(2):
                    evac4(2 * c + j, st[j], *r[j])
                yield

            tk = [None] * 4
            drain(two_chunks(f"{tag}g0", f"{tag}u0", bank[0:4], xk, xtok, tk))
            x_norm_a()
            pend = None
            for c in range(1, NF // 2):
                bs = bank[4:8] if c % 2 else bank[0:4]
                t2 = []
                ga = tiles(f"{tag}g{c}", bs[0:2], xk, xtok, toks=t2)
                if c == 1:
                    next(ga)
                    x_norm_b()
                    barrier(snap)
                    pend = evac_pair(0, bank[0:4], tk)
                both(ga, pend, 1)
                both(tiles(f"{tag}u{c}", bs[2:4], xk, xtok, toks=t2), pend, 1)
                drain(pend)
                pend = evac_pair(c, bs, t2)
            drain(pend)
            rb.free = q.now()

            def ak(k):
                return AH[:, k, :], AL[:, k, :]

            for p in range(4):
                bs = bank[2 * p:2 * p + 2]
                tk = []
                drain(tiles(f"{tag}d{p}", bs, ak, atok, toks=tk, nu=6))
                for j in range(2):
                    resid(2 * p + j, bs[j], tk[j], 0.25, gnext)

        def split_scaled(src, h, l, scale, waits, free=()):
            t1 = put("act", lambda e: e.activation(h, src, ACT.Copy, scale=scale), waits, free)
            if isinstance(scale, float) and scale == 1.0:
                t2 = put("dve", lambda e: e.tensor_tensor(l, src, F(h), ALU.subtract), t1, waits, free)
            else:
                t2 = put("dve", lambda e: e.scalar_tensor_tensor(l, src, scale, F(h), ALU.mult, ALU.subtract), t1, waits, free)
            return [t1, t2]

        def split_bank(parts, waits, free=()):
            for src, h, l, sc in parts:
                t1 = put("act", lambda e, src=src, h=h, sc=sc: e.activation(h, src, ACT.Copy, scale=sc), waits, free)
            for src, h, l, sc in parts:
                t2 = put("dve", lambda e, src=src, h=h, l=l, sc=sc: e.scalar_tensor_tensor(l, src, sc, F(h), ALU.mult, ALU.subtract),
                         t1, waits, free)
            return [t1, t2]

        def evac_rb(b, tok, s, h, l, scale, free=()):
            t = put("dve", lambda e: e.tensor_tensor(s.ap, b.ap[:, :], RB[:, :], ALU.mult), tok, rbt["rb"], s.free)
            b.free = [t]
            r = split_scaled(s.ap, h, l, scale, [t], free)
            s.free = r
            return r

        def v_chunk(name, banks, lhs, ltok, nt, toks):
            w0, w1 = get((name, 0)), get((name, 1))
            for i in range(nt):
                b = banks[i // 2]
                for k in range(KT):
                    w = w0 if k < 4 else w1
                    lh, ll = lhs(k)
                    o = b.ap[:, (i % 2) * 256:(i % 2) * 256 + 256]
                    sl = slice(i * 128, i * 128 + 128)
                    t = mm3(o, lh[:, sl], ll[:, sl], w[0][:, k % 4, :], w[1][:, k % 4, :],
                            [w[2], ltok[k] if ltok else None, b.free if i % 2 == 0 and k == 0 else None],
                            k == 0, k == 7, mark=k == 7)
                toks.append(t)
                if i == nt - 1:
                    done(w0, t)
                    done(w1, t)
                    pump()
                yield

        def evac_v(banks, toks, vh, vl, nt, scaled, free):
            r = []
            for n in range(nt // 2):
                b = banks[n]
                parts = [(b.ap[:, j * 256:j * 256 + 256], vh[:, 2 * n + j, :], vl[:, 2 * n + j, :],
                          RCOL[:, 2 * n + j:2 * n + j + 1] if scaled else 1.0) for j in range(2)]
                b.free = split_bank(parts, [toks[2 * n + 1], rbt["rcol"] if scaled else None], free)
                r += b.free
            return r

        def pT_views(off):
            h = AR[:, off:off + 1536].rearrange("p (j t) -> p j t", t=256)
            l = AR[:, off + 1536:off + 3072].rearrange("p (j t) -> p j t", t=256)
            return h, l

        def clear_pT(PH, PL):
            toks = []
            for j in (1, 5):
                for P_ in (PH, PL):
                    toks.append(put("dve", lambda e, P_=P_, j=j: e.memset(F(P_[:, j, 0:128]), 0.0)))
            return toks

        def softmax_row(sbk, n, tok, p, cq, mxc):
            mx, nb, ls = MX[:, mxc:mxc + 1], NB[:, mxc:mxc + 1], LS[:, mxc:mxc + 1]
            t1 = put("dve", lambda e: e.reduce_max(mx, sbk.ap[:, 0:n], AX), tok, smf[mxc])
            if cq is None:
                t2 = put("dve", lambda e: e.tensor_scalar(nb, mx, -1.0, None, ALU.mult), t1, smf[mxc])
            else:
                t2 = put("dve", lambda e: e.scalar_tensor_tensor(nb, mx, cq, cq, ALU.add, ALU.subtract, reverse1=True), t1, smf[mxc])
            t3 = put("act", lambda e: e.activation(p.ap[:, 0:n], sbk.ap[:, 0:n], ACT.Exp, bias=nb, accum_out=ls), t2, p.free, smf[mxc])
            sbk.free = [t3]
            smf[mxc] = [t3]
            return t3, ls

        smf = [[], [], [], []]

        def shape_matrix(dst, col, snap):
            s = S[3]
            d = put("sp", lambda e: e.dma_start(s.ap[:, 0:128], consts[:, col:col + 128]), s.free, sem="c0", by=16)
            t = put("act", lambda e: e.activation(dst, s.ap[:, 0:128], ACT.Copy), d, snap)
            s.free = [t]
            return t

        def plan_mix(l):
            w, wo = a["w_mix_in"][l], a["w_mix_out"][l]
            t = f"m{l}"
            plan_cols(t + "q0", w, 3 * CW)
            plan_cols(t + "k0", w, 4 * CW)
            plan_cols(t + "v0", w, 5 * CW)
            plan((t + "zf", 0), w[:, 6 * CW:6 * CW + 8].rearrange("(k p) c -> p k c", p=128), kind="pad")
            for h in range(2):
                if h == 1:
                    plan_cols(t + "q1", w, 3 * CW + 256)
                    plan_cols(t + "k1", w, 4 * CW + 256)
                plan_cols(t + f"zc{h}", w, CW + h * 256)
                plan_cols(t + f"zv{h}", w, 2 * CW + h * 256)
                plan_cols(t + f"zb{h}", w, h * 256)
                if h == 0:
                    plan_cols(t + "v1", w, 5 * CW + 256)
            for p in range(4):
                plan_cols(t + f"o{p}", wo, p * 256)

        def mix(l, snap, gnext, mem_side):
            tg = f"m{l}"
            gco, gat = 80 + 4 * l, 88 + 4 * l
            YH = AR[:, 0:4096].rearrange("p (k t) -> p k t", t=T)
            YL = AR[:, 4096:8192].rearrange("p (k t) -> p k t", t=T)
            QK = AR[:, 8192:12288].rearrange("p (k t) -> p k t", t=T)
            QH, QL, KH, KL = QK[:, 0:2], QK[:, 2:4], QK[:, 4:6], QK[:, 6:8]
            VV = AR[:, 12288:16384].rearrange("p (s i c) -> p s i c", s=4, c=256)
            PH, PL = pT_views(16384)
            NCH, NCL = AR[0:8, 19456:19968], AR[0:8, 19968:20480]
            CB = [Buf(AF[:, i * T:i * T + T]) for i in range(2)]
            UB = [Buf(AF[:, 1024 + i * 514:1024 + i * 514 + 514]) for i in range(2)]
            RBC, RBA = AF[:, 2052:2564], AF[:, 2564:3076]
            CQ = AF[:, 3076:3108].rearrange("p (i h) -> p i h", h=8)
            tk = [None] * 4
            drain(two_chunks(tg + "q0", tg + "k0", bank[0:4], xk, xtok, tk))
            x_norm_a()
            vt = []
            g = v_chunk(tg + "v0", bank[4:6], xk, xtok, 4, vt)
            next(g)
            x_norm_b()
            drain(g)
            barrier(snap)
            MR = AR[:, 20480:20608]
            mrt = shape_matrix(MR, C_MQ, snap)
            ztok = clear_pT(PH, PL)
            for i in range(2):
                ztok.append(put("dve", lambda e, i=i: e.memset(UB[i].ap[:, 0:2], 0.0)))
            qkt = {}
            for i in range(4):
                h, lo = ((QH, QL), (KH, KL))[i // 2]
                qkt[i] = evac_rb(bank[i], tk[i], S[i % 2], h[:, i % 2, :], lo[:, i % 2, :], 0.125 if i < 2 else 1.0)
            vtok = [None, None]
            vtok[0] = evac_v(bank[4:6], vt, VV[:, 0], VV[:, 1], 4, True, ())
            w = get((tg + "zf", 0))
            for k in range(KT):
                t = mm3(bank[7].ap[:, :], w[0][:, k, :], w[1][:, k, :], XH[:, k, :], XL[:, k, :],
                        [w[2], xtok[k], bank[7].free if k == 0 else None], k == 0, k == 7, mark=k == 7)
            done(w, t)
            pump()
            z, y, on = S[2], S[3], S[4]
            z8, y8, o8 = z.ap[0:8, :], y.ap[0:8, :], on.ap[0:8, :]
            t0 = put("dve", lambda e: e.memset(o8, 1.0), on.free)
            t = put("dve", lambda e: e.tensor_tensor(z8, bank[7].ap[0:8, :], RB[0:8, :], ALU.mult), t, rbt["rb"], z.free)
            bank[7].free = [t]
            t = put("dve", lambda e: e.tensor_scalar(z8, z8, BF[0:8, l:l + 1], None, ALU.add), t)
            t1 = put("act", lambda e: e.activation(y8, z8, ACT.Abs), t, y.free)
            t1 = put("act", lambda e: e.activation(y8, y8, ACT.Exp, scale=-1.0), t1)
            t1 = put("act", lambda e: e.activation(y8, y8, ACT.Ln, bias=1.0), t1)
            t = put("dve", lambda e: e.scalar_tensor_tensor(z8, z8, 0.0, y8, ALU.min, ALU.subtract), t1, t)
            tc = put("dve", lambda e: e.tensor_tensor_scan(y8, o8, z8, 0.0, ALU.mult, ALU.add), t, t0, t1)
            nct = split_scaled(y8, NCH, NCL, -1.0, [tc])
            drain_main = chain(*[])
            for i in range(4):
                tt = pe_transpose(bank[6].ap[:, i * 8:i * 8 + 8], y8[:, i * 128:(i + 1) * 128], ID[0:8, 0:8],
                                  [tc, bank[6].free if i == 0 else None], i == 3)
            tcq = put("dve", lambda e: e.tensor_copy(CQ[:, :, :], bank[6].ap[:, 0:32].rearrange("p (i h) -> p i h", h=8)), tt)
            bank[6].free = [tcq]
            z.free, y.free, on.free = [tc], [nct, tt], [tc]

            ytok = [None] * 8
            qkfree = []
            vfree = []
            st = {"acc": None, "pv": None}

            def att(quad):
                A_ = {}
                ev = {}

                def stage_a(n):
                    hq, i = divmod(n, 4)
                    tl, hh = divmod(hq, 2)
                    h = 4 * quad + hq
                    r = slice(64 * hh, 64 * hh + 64)
                    N = (i + 1) * 128
                    b = bank[4 + n % 2]
                    o = b.ap[:, 0:N]
                    qs = slice(i * 128, N)
                    mm3(o, QH[r, tl, qs], QL[r, tl, qs], KH[r, tl, 0:N], KL[r, tl, 0:N],
                        [qkt[tl], qkt[2 + tl], b.free], True, False)
                    e8 = IDR[0:8, h:h + 1].to_broadcast([8, 128])
                    mm(o, e8, NCH[:, 0:N], [nct], False, False, False)
                    mm(o, e8, NCL[:, 0:N], (), False, False, False)
                    t = mm(b.ap[:, N - 128:N], IDR[:, :], MR, [mrt], False, True, True)
                    qkfree.append(t)
                    p = S[2 + n % 2]
                    t3, ls = softmax_row(b, N, t, p, CQ[:, i, h:h + 1], n % 2)
                    rl = RL[:, n % 2:n % 2 + 1]
                    t4 = put("dve", lambda e: e.reciprocal(rl, ls), t3)
                    smf[n % 2] = [t3, t4]
                    t5 = put("dve", lambda e: e.tensor_scalar(p.ap[:, 0:N], p.ap[:, 0:N], rl, None, ALU.mult), t4, t3)
                    A_[n] = (p, t5, N)

                def stage_b(n):
                    hq, i = divmod(n, 4)
                    p, tp, N = A_.pop(n)
                    b = bank[6]
                    for j in range(i + 1):
                        t = pe_transpose(b.ap[:, j * 128:(j + 1) * 128], p.ap[:, j * 128:(j + 1) * 128], ID,
                                         [tp, b.free if j == 0 else None], j == i)
                    p.free = [t]
                    j0 = 0 if i < 2 else 2
                    src = b.ap[:, 0:N].rearrange("p (j t) -> p j t", t=128)
                    cs = slice((i % 2) * 128, (i % 2) * 128 + 128)
                    r = split_scaled(src, PH[:, j0:j0 + i + 1, cs], PL[:, j0:j0 + i + 1, cs], 1.0, [t], [st["pv"], ztok])
                    b.free = r
                    ev[n] = r

                def stage_c(hq):
                    tl, hh = divmod(hq, 2)
                    b = bank[7]
                    for a_ in range(2):
                        for j in range(2 * a_ + 2):
                            jj = (0 if a_ == 0 else 2) + j
                            t = mm3(b.ap[:, a_ * 256:a_ * 256 + 256], VV[:, 2 * quad, j, tl * 128:tl * 128 + 128],
                                    VV[:, 2 * quad + 1, j, tl * 128:tl * 128 + 128], PH[:, jj, :], PL[:, jj, :],
                                    [vtok[quad], ev[4 * hq + 2 * a_ + 1], ev[4 * hq + 2 * a_], b.free if j == 0 and a_ == 0 else None],
                                    j == 0, j == 2 * a_ + 1, mark=j == 2 * a_ + 1)
                    st["pv"] = t
                    r = slice(64 * hh, 64 * hh + 64)
                    kt = 4 + 2 * quad + tl
                    src = b.ap[r, :]
                    g_ = GA[r, gat + kt - 4:gat + kt - 3]
                    if kt == 4:
                        ts = put("act", lambda e: e.activation(RBA[r, :], src, ACT.Square), t)
                        st["acc%d" % hh] = ts
                    else:
                        sq = S[5]
                        ts = put("act", lambda e: e.activation(sq.ap[r, :], src, ACT.Square), t, sq.free)
                        ta = put("pool", lambda e: e.tensor_tensor(RBA[r, :], RBA[r, :], sq.ap[r, :], ALU.add), ts, st["acc%d" % hh])
                        sq.free = [ta]
                        st["acc%d" % hh] = ta
                    rr = split_scaled(src, YH[r, kt, :], YL[r, kt, :], g_, [t])
                    b.free = [ts, rr]
                    ytok[kt] = [ytok[kt], rr]

                for n in range(18):
                    if n < 16:
                        stage_a(n)
                    yield
                    if n >= 2 and (n - 2) % 4 == 3:
                        stage_c((n - 2) // 4)
                        yield
                    if 1 <= n <= 16:
                        stage_b(n - 1)
                        yield

            accc = {}

            def conv(half, side, per):
                tks = []
                both(tiles(tg + f"zc{half}", bank[0:2], xk, xtok, toks=tks), side, per)
                ct = []
                for j in range(2):
                    t = put("dve", lambda e, j=j: e.tensor_tensor(CB[j].ap, bank[j].ap[:, :], RB[:, :], ALU.mult), tks[j], CB[j].free)
                    bank[j].free = [t]
                    ct.append(t)
                tks = []
                both(tiles(tg + f"zv{half}", bank[2:4], xk, xtok, toks=tks), side, per)
                for j in range(2):
                    m = 2 * half + j
                    wc = [GB[:, (l * 3 + kk) * 4 + m:(l * 3 + kk) * 4 + m + 1] for kk in range(3)]
                    s, u, c = S[j], UB[j], CB[j]
                    t = put("dve", lambda e: e.tensor_tensor(s.ap, bank[2 + j].ap[:, :], RB[:, :], ALU.mult), tks[j], s.free)
                    bank[2 + j].free = [t]
                    t = put("dve", lambda e: e.tensor_tensor(u.ap[:, 2:514], s.ap, c.ap, ALU.mult), t, ct[j], u.free)
                    s.free = [t]
                    t = put("dve", lambda e: e.tensor_scalar(c.ap, u.ap[:, 2:514], wc[2], None, ALU.mult), t, ztok)
                    t = put("dve", lambda e: e.scalar_tensor_tensor(c.ap, u.ap[:, 1:513], wc[1], c.ap, ALU.mult, ALU.add), t)
                    t = put("dve", lambda e: e.scalar_tensor_tensor(c.ap, u.ap[:, 0:512], wc[0], c.ap, ALU.mult, ALU.add), t)
                    u.free = [t]
                    ct[j] = t
                tks = []
                both(tiles(tg + f"zb{half}", bank[0:2], xk, xtok, toks=tks), side, per)
                for j in range(2):
                    m = 2 * half + j
                    s, c = S[j], CB[j]
                    t = put("dve", lambda e: e.tensor_tensor(s.ap, bank[j].ap[:, :], RB[:, :], ALU.mult), tks[j], s.free)
                    bank[j].free = [t]
                    t = put("dve", lambda e: e.tensor_tensor(s.ap, s.ap, c.ap, ALU.mult), t, ct[j])
                    c.free = [t]
                    rr = split_scaled(s.ap, YH[:, m, :], YL[:, m, :], GA[:, gco + m:gco + m + 1], [t])
                    ytok[m] = rr
                    if m == 0:
                        ts = put("act", lambda e: e.activation(RBC, s.ap, ACT.Square), t)
                        accc["t"] = ts
                    else:
                        sq = S[4]
                        ts = put("act", lambda e: e.activation(sq.ap, s.ap, ACT.Square), t, sq.free)
                        ta = put("pool", lambda e: e.tensor_tensor(RBC, RBC, sq.ap, ALU.add), ts, accc["t"])
                        sq.free = [ta]
                        accc["t"] = ta
                    s.free = [rr, ts]

            side = att(0)
            conv(0, side, 5)
            vt = []
            both(v_chunk(tg + "v1", bank[2:4], xk, xtok, 4, vt), side, 4)
            vtok[1] = evac_v(bank[2:4], vt, VV[:, 2], VV[:, 3], 4, True, ())
            drain(side)
            for nm, bb, (h, lo), sc_, key in (("q1", 0, (QH, QL), 0.125, 0), ("k1", 2, (KH, KL), 1.0, 2)):
                tks = []
                drain(tiles(tg + nm, bank[bb:bb + 2], xk, xtok, toks=tks))
                for j in range(2):
                    qkt[key + j] = evac_rb(bank[bb + j], tks[j], S[j], h[:, j, :], lo[:, j, :], sc_, list(qkfree))
            side = att(1)
            conv(1, side, 6)
            rb.free = q.now()

            def norm_y(buf, acct, bk, r4):
                r, t = inv_rms(bk, 1, CW, acct, lambda i: buf[:, i * 128:(i + 1) * 128], ONE, r4, r4.ap, 1)
                pe = q.now()[:1]
                return t, pe

            def norm_y2(buf, bk, r4, t, pe):
                t = spread(bk, r4, r4.ap, t)
                t = put("act", lambda e: e.activation(buf, bk.ap[:, :], ACT.Copy), t, pe)
                bk.free = [t]
                return t

            def half(p, u, bs, k0):
                w = get((tg + f"o{p}", u))
                toks = []
                for k in range(4):
                    kk = k0 + k
                    for c in range(2):
                        b = bs[c]
                        t = mm3(b.ap[:, :], w[0][:, k, c * 128:(c + 1) * 128], w[1][:, k, c * 128:(c + 1) * 128],
                                YH[:, kk, :], YL[:, kk, :], [w[2], ytok[kk], b.free if k == 0 else None], k == 0, k == 3, mark=k == 3)
                        if k == 3:
                            toks.append(t)
                    if k in (1, 3):
                        if k == 3:
                            done(w, t)
                            pump()
                        res[(p, u)] = toks
                        yield

            res = {}
            both(half(0, 0, bank[0:2], 0), side, 6)
            nc0 = norm_y(RBC, accc["t"], bank[2], S[4])
            both(half(1, 0, bank[2:4], 0), side, 8)
            drain(side)
            rc = norm_y2(RBC, bank[6], S[4], *nc0)
            na0 = norm_y(RBA, [st["acc0"], st["acc1"]], bank[7], S[5])
            drain(half(0, 1, bank[4:6], 4))
            ra = norm_y2(RBA, bank[6], S[5], *na0)

            def evac_o(m):
                bc, ba = bank[m % 4], bank[4 + m % 4]
                p = m // 2
                s0, s1 = S[2 * (m % 2)], S[2 * (m % 2) + 1]
                t = put("dve", lambda e: e.tensor_tensor(s0.ap, bc.ap[:, :], RBC, ALU.mult), res[(p, 0)][m % 2], rc, s0.free)
                bc.free = [t]
                t2 = put("dve", lambda e: e.tensor_tensor(s1.ap, ba.ap[:, :], RBA, ALU.mult), res[(p, 1)][m % 2], ra, s1.free)
                ba.free = [t2]
                t = put("dve", lambda e: e.tensor_tensor(X[:, m, :], X[:, m, :], s0.ap, ALU.add), t)
                s0.free = [t]
                t = put("dve", lambda e: e.tensor_tensor(X[:, m, :], X[:, m, :], s1.ap, ALU.add), t, t2)
                s1.free = [t]
                x_post(m, t, gnext)

            evac_o(0)
            evac_o(1)
            next(mem_side, None)
            drain(half(1, 1, bank[6:8], 4))
            evac_o(2)
            evac_o(3)
            drain(mem_side)
            drain(half(2, 0, bank[0:2], 0))
            drain(half(2, 1, bank[4:6], 4))
            evac_o(4)
            evac_o(5)
            drain(half(3, 0, bank[2:4], 0))
            drain(half(3, 1, bank[6:8], 4))
            evac_o(6)
            evac_o(7)

        MH = AR[:, 8192:10240].rearrange("p (k t) -> p k t", t=256)
        ML = AR[:, 10240:12288].rearrange("p (k t) -> p k t", t=256)
        mtok = [None] * KT

        def mem_prep(l, gmem):
            us = [get((f"mem{l}", r)) for r in range(2)]
            s = S[0]
            nt = []
            for r in range(2):
                ap, tok, _ = us[r]
                row = ap.rearrange("p k c -> p (k c)")
                ts = []
                for hf in range(2):
                    ts.append(put("act", lambda e, r=r, hf=hf, row=row: e.activation(s.ap, row[:, hf * 512:hf * 512 + 512], ACT.Square,
                                  accum_out=MSS[:, 2 * r + hf:2 * r + hf + 1]), tok, s.free, ts))
                s.free = [ts]
                t = put("dve", lambda e, r=r: e.tensor_tensor(MS[:, r:r + 1], MSS[:, 2 * r:2 * r + 1], MSS[:, 2 * r + 1:2 * r + 2], ALU.add), ts, pwfree["ms"])
                t = put("dve", lambda e, r=r: e.tensor_scalar(MS[:, r:r + 1], MS[:, r:r + 1], 1.0 / D, EPS, ALU.mult, ALU.add), t)
                t = put("pool", lambda e, r=r: e.tensor_tensor(PW[:, r:r + 1], MS[:, r:r + 1], NH[:, 0:1], ALU.pow), t, pwfree["pw"])
                t = put("dve", lambda e, r=r, row=row: e.tensor_scalar(row, row, PW[:, r:r + 1], None, ALU.mult), t, ts)
                nt.append(t)
            pwfree["ms"] = [t]
            pwfree["pw"] = [t]
            yield
            b = bank[6]
            for k2 in range(4):
                bb = bank[6 + k2 % 2]
                for j in range(2):
                    for r in range(2):
                        row = us[r][0].rearrange("p k c -> p (k c)")
                        k = 2 * k2 + j
                        t = pe_transpose(bb.ap[:, j * 256 + r * 128:j * 256 + r * 128 + 128], row[:, k * 128:(k + 1) * 128], ID,
                                         [nt, bb.free if j == 0 and r == 0 else None], j == 1 and r == 1)
                bb.free = split_bank([(bb.ap[:, j * 256:j * 256 + 256], MH[:, 2 * k2 + j, :], ML[:, 2 * k2 + j, :],
                                       GA[:, gmem + 2 * k2 + j:gmem + 2 * k2 + j + 1]) for j in range(2)], [t])
                mtok[2 * k2] = mtok[2 * k2 + 1] = bb.free
                if k2 == 3:
                    for r in range(2):
                        raw_done(us[r], [t, nt[r]])
                    pump()
                yield

        def plan_x(l):
            wq, wkv, wo = a["w_xq"][l], a["w_xkv"][l], a["w_xo"][l]
            for h in range(4):
                plan_cols(f"x{l}k{h}", wkv, h * 256)
                plan_cols(f"x{l}v{h}", wkv, D + h * 256)
                plan_cols(f"x{l}q{h}", wq, h * 256)
            for p in range(4):
                plan_cols(f"x{l}o{p}", wo, p * 256)

        def xattn(l, snap, gnext):
            tg = f"x{l}"
            OH = AR[:, 0:4096].rearrange("p (k t) -> p k t", t=T)
            OL = AR[:, 4096:8192].rearrange("p (k t) -> p k t", t=T)
            KV = AR[:, 12288:16384].rearrange("p (s i c) -> p s i c", s=8, c=256)
            QX = AR[:, 16384:20480].rearrange("p (s t) -> p s t", t=T)
            PT = AR[:, 20480:22528].rearrange("p (s t) -> p s t", t=T)
            PH, PL = PT[:, 0:2, :], PT[:, 2:4, :]
            otok = [None] * 8
            st = {"pv": None, "sc": [None, None], "vr": [None, None]}
            hd = {}

            def att(h):
                par = h % 2
                KH, KL, VH, VL = (KV[:, 4 * par + j] for j in range(4))
                QH, QL = QX[:, 4 * par:4 * par + 2, :], QX[:, 4 * par + 2:4 * par + 4, :]
                A_, ev = {}, {}

                def stage_a(i):
                    b = bank[4 + i % 2]
                    qs = slice(i * 128, i * 128 + 128)
                    for d in range(2):
                        t = mm3(b.ap[:, 0:256], QH[:, d, qs], QL[:, d, qs], KH[:, d, :], KL[:, d, :],
                                [hd[h]["q"], hd[h]["k"], b.free], d == 0, d == 1, mark=d == 1)
                    st["sc"][par] = t
                    p = S[2 + i % 2]
                    t3, ls = softmax_row(b, 256, t, p, None, i % 2)
                    rl = RL[:, i % 2:i % 2 + 1]
                    t4 = put("dve", lambda e: e.reciprocal(rl, ls), t3)
                    smf[i % 2] = [t3, t4]
                    t5 = put("dve", lambda e: e.tensor_scalar(p.ap[:, 0:256], p.ap[:, 0:256], rl, None, ALU.mult), t4, t3)
                    A_[i] = (p, t5)

                def stage_b(i):
                    p, tp = A_[i]
                    b = bank[6]
                    for j in range(2):
                        t = pe_transpose(b.ap[:, j * 128:(j + 1) * 128], p.ap[:, j * 128:(j + 1) * 128], ID,
                                         [tp, b.free if j == 0 else None], j == 1)
                    p.free = [t]
                    src = b.ap[:, 0:256].rearrange("p (j t) -> p j t", t=128)
                    qs = slice(i * 128, i * 128 + 128)
                    ev[i] = split_scaled(src, PH[:, :, qs], PL[:, :, qs], 1.0, [t], [st["pv"]])
                    b.free = ev[i]

                def stage_c(d):
                    b = bank[7]
                    for j in range(2):
                        t = mm3(b.ap[:, :], VH[:, j, d * 128:(d + 1) * 128], VL[:, j, d * 128:(d + 1) * 128], PH[:, j, :], PL[:, j, :],
                                [hd[h]["v"], list(ev.values()), b.free if j == 0 else None], j == 0, j == 1, mark=j == 1)
                    if d == 1:
                        st["pv"] = t
                        st["vr"][par] = t
                    rr = split_scaled(b.ap[:, :], OH[:, 2 * h + d, :], OL[:, 2 * h + d, :], 1.0, [t])
                    b.free = rr
                    otok[2 * h + d] = rr

                for n in range(5):
                    if n < 4:
                        stage_a(n)
                        yield
                    if n >= 1:
                        stage_b(n - 1)
                        yield
                stage_c(0)
                yield
                stage_c(1)
                yield

            side = iter(())
            for h in range(4):
                par = h % 2
                KH, KL, VH, VL = (KV[:, 4 * par + j] for j in range(4))
                QH, QL = QX[:, 4 * par:4 * par + 2, :], QX[:, 4 * par + 2:4 * par + 4, :]
                tk = []
                both(tiles(tg + f"k{h}", bank[0:2], lambda k: (MH[:, k, :], ML[:, k, :]), mtok, toks=tk, n=256), side, 2)
                if h == 0:
                    x_norm_a()
                    barrier(snap)
                hd[h] = {"k": []}
                for j in range(2):
                    r = split_scaled(bank[j].ap[:, 0:256], KH[:, j, :], KL[:, j, :], 1.0, [tk[j]], [st["sc"][par]])
                    bank[j].free = r
                    hd[h]["k"] += r
                vt = []
                both(v_chunk(tg + f"v{h}", bank[2:3], lambda k: (MH[:, k, :], ML[:, k, :]), mtok, 2, vt), side, 2)
                if h == 0:
                    x_norm_b()
                hd[h]["v"] = evac_v(bank[2:3], vt, VH, VL, 2, False, [st["vr"][par]])
                tk = []
                both(tiles(tg + f"q{h}", bank[0:2], xk, xtok, toks=tk), side, 2)
                drain(side)
                hd[h]["q"] = [evac_rb(bank[j], tk[j], S[j], QH[:, j, :], QL[:, j, :], 1.0 / 16.0, [st["sc"][par]]) for j in range(2)]
                side = att(h)
            rb.free = q.now()

            def ok(k):
                return OH[:, k, :], OL[:, k, :]

            out_proj(tg, ok, otok, gnext, side)

        def out_proj(tg, ok, otok, gnext, side, fin=False):
            tk = [None] * 4
            g = two_chunks(tg + "o0", tg + "o1", bank[0:4], ok, otok, tk)
            for _ in range(4):
                next(g)
                for _ in range(4):
                    next(side, None)
            drain(side)
            drain(g)
            for m in range(4):
                resid(m, bank[m], tk[m], 1.0, gnext) if not fin else fin_tile(m, bank[m], tk[m])
            for p in (2, 3):
                bs = bank[2 * p:2 * p + 2]
                tk = []
                drain(tiles(tg + f"o{p}", bs, ok, otok, toks=tk))
                for j in range(2):
                    m = 2 * p + j
                    resid(m, bs[j], tk[j], 1.0, gnext) if not fin else fin_tile(m, bs[j], tk[j])

        def fin_tile(m, b, tok):
            tx = put("dve", lambda e: e.scalar_tensor_tensor(X[:, m, :], b.ap[:, :], 1.0, X[:, m, :], ALU.mult, ALU.add), tok)
            b.free = [tx]
            xlast[m] = tx

        xlast = [None] * KT

        def store(snap):
            outs = []
            for i in range(4):
                for hf in range(2):
                    n = 2 * i + hf
                    b = bank[n % 4]
                    for j in range(4):
                        m = 4 * hf + j
                        t = pe_transpose(b.ap[:, j * 128:(j + 1) * 128], X[:, m, i * 128:(i + 1) * 128], ID,
                                         [snap, xlast[m], b.free if j == 0 else None], j == 3)
                    s = S[n % NS]
                    if n % 2:
                        t = put("act", lambda e, s=s, b=b: e.activation(s.ap, b.ap[:, :], ACT.Copy), t, s.free)
                    else:
                        t = put("dve", lambda e, s=s, b=b: e.tensor_copy(s.ap, b.ap[:, :]), t, s.free)
                    b.free = [t]
                    dst = out[0, i * 128:(i + 1) * 128, hf * 512:hf * 512 + 512]
                    tw = put("sp", lambda e, s=s, dst=dst: e.dma_start(dst, s.ap), t, sem=f"out{n % NS}", by=16)
                    s.free = [tw]
                    outs.append(tw)
            q.hold("sp", outs)

        def plan_diff():
            w, wo = a["a_w_in_2"][0], a["a_w_out_2"][0]
            plan_cols("dq0", w, 0)
            plan_cols("dk0", w, D)
            plan_cols("dv0", w, 2 * D)
            plan_cols("dg0", w, 3 * D)
            for t in range(1, 4):
                for i, nm in ((2, "v"), (3, "g"), (0, "q"), (1, "k")):
                    plan_cols(f"d{nm}{t}", w, i * D + t * 256)
            for p in range(4):
                plan_cols(f"do{p}", wo, p * 256)

        def gate_evac(bs, tk, G, gfree, tmp):
            r = []
            for j in range(2):
                t = put("dve", lambda e, j=j: e.tensor_tensor(G[j], bs[j].ap[:, :], RB[:, :], ALU.mult), tk[j], rbt["rb"], gfree)
                bs[j].free = [t]
                t1 = put("act", lambda e, j=j: e.activation(tmp.ap, G[j], ACT.Tanh, scale=0.5), t, tmp.free)
                t2 = put("dve", lambda e, j=j: e.scalar_tensor_tensor(G[j], tmp.ap, 1.0, G[j], ALU.add, ALU.mult), t1, t)
                tmp.free = [t2]
                r.append(t2)
            return r

        def diff(snap, gnext):
            OH = AR[:, 0:4096].rearrange("p (k t) -> p k t", t=T)
            OL = AR[:, 4096:8192].rearrange("p (k t) -> p k t", t=T)
            QK = AR[:, 8192:12288].rearrange("p (k t) -> p k t", t=T)
            QH, QL, KH, KL = QK[:, 0:2], QK[:, 2:4], QK[:, 4:6], QK[:, 6:8]
            VV = AR[:, 12288:16384].rearrange("p (s i c) -> p s i c", s=4, c=256)
            PH, PL = pT_views(16384)
            G = [AF[:, i * T:i * T + T] for i in range(4)]
            COS, SIN = AF[:, 2048:2560], AF[:, 2560:3072]
            tk = [None] * 4
            drain(two_chunks("dq0", "dk0", bank[0:4], xk, xtok, tk))
            x_norm_a()
            vt = []
            g = v_chunk("dv0", bank[4:6], xk, xtok, 4, vt)
            next(g)
            x_norm2_a()
            drain(g)
            x_norm2_b()
            barrier(snap)
            ct = [put("sp", lambda e: e.dma_start(AF[:, 2048:3072], consts[:, C_COS:C_COS + 2 * T]), snap, sem="c1", by=16)]
            MR = AR[:, 19456:19584]
            mrt = shape_matrix(MR, C_MQ, snap)
            ROT = AR[:, 19584:19712]
            rott = shape_matrix(ROT, C_ROT, snap)
            ztok = clear_pT(PH, PL)
            qkt = [None] * 4
            qkfree = []
            vtok = [None] * 4
            gtok = [None] * 4
            vtok[0] = evac_v(bank[4:6], vt, VV[:, 0], VV[:, 1], 4, True, ())
            st = {"pv": None, "prev": []}
            gfree = [[], []]
            otok = [None] * 8

            def qk_chain(which, bs, tk, gain):
                H_, L_ = ((QH, QL), (KH, KL))[which]
                tp = S[2]
                tq = []
                for j in range(2):
                    s = S[j]
                    t = put("dve", lambda e, j=j, s=s: e.tensor_tensor(s.ap, bs[j].ap[:, :], RB[:, :], ALU.mult), tk[j], rbt["rb"], s.free)
                    bs[j].free = [t]
                    tq.append(t)
                yield
                for j in range(2):
                    s = S[j]
                    t = put("act", lambda e, s=s: e.activation(tp.ap, s.ap, ACT.Square), tq[j], tp.free)
                    yield
                    for i in range(4):
                        t1 = mm(bs[j].ap[:, i * 2:i * 2 + 2], tp.ap[:, i * 128:(i + 1) * 128], BLK, [t, bs[j].free if i == 0 else None], mark=i == 3)
                    yield
                    t2 = put("dve", lambda e, j=j: e.tensor_scalar(MS[:, 0:8], bs[j].ap[:, 0:8], 1.0 / 64, EPS, ALU.mult, ALU.add), t1, pwfree["ms"])
                    t3 = put("pool", lambda e: e.tensor_tensor(PW[:, 0:8], MS[:, 0:8], NH[:, 0:8], ALU.pow), t2, pwfree["pw"])
                    pwfree["ms"] = [t3]
                    src = PW[:, 0:8].unsqueeze(2).to_broadcast([128, 8, 64])
                    t4 = put("dve", lambda e: e.tensor_copy(tp.ap.rearrange("p (g w) -> p g w", w=64), src), t3, t1)
                    pwfree["pw"] = [t4]
                    bs[j].free = [t2]
                    yield
                    for i in range(4):
                        t5 = pe_transpose(bs[j].ap[:, i * 128:(i + 1) * 128], tp.ap[:, i * 128:(i + 1) * 128], ID,
                                          [t4, bs[j].free if i == 0 else None], i == 3)
                    t6 = put("dve", lambda e, j=j, s=s: e.scalar_tensor_tensor(s.ap, s.ap, gain, bs[j].ap[:, :], ALU.mult, ALU.mult), t5, tq[j])
                    yield
                    t7 = mm(bs[j].ap[:, :], F(ROT), s.ap, [t6, rott])
                    t8 = put("pool", lambda e, s=s: e.tensor_tensor(tp.ap, s.ap, COS, ALU.mult), t6, t5, ct)
                    yield
                    t9 = put("dve", lambda e, j=j, s=s: e.tensor_tensor(s.ap, bs[j].ap[:, :], SIN, ALU.mult), t7, t8)
                    bs[j].free = [t9]
                    t10 = put("dve", lambda e, s=s: e.tensor_tensor(s.ap, s.ap, tp.ap, ALU.add), t9)
                    tp.free = [t10]
                    r = split_scaled(s.ap, H_[:, j, :], L_[:, j, :], 1.0, [t10], st["prev"])
                    s.free = r
                    qkt[2 * which + j] = r
                    yield

            def att(pair):
                A_, ev = {}, {}
                mine = []

                def stage_a(n):
                    hq, i = divmod(n, 4)
                    N = (i + 1) * 128
                    qs = slice(i * 128, N)
                    ts = []
                    for c in range(2):
                        r = slice(64 * c, 64 * c + 64)
                        b = bank[4 + c]
                        o = b.ap[:, 0:N]
                        mm3(o, QH[r, hq, qs], QL[r, hq, qs], KH[r, hq, 0:N], KL[r, hq, 0:N],
                            [qkt[hq], qkt[2 + hq], b.free], True, False)
                        t = mm(b.ap[:, N - 128:N], IDR[:, :], MR, [mrt], False, True, True)
                        mine.append(t)
                        ts.append(t)
                    A_[n] = ts

                def stage_a2(n):
                    N = (n % 4 + 1) * 128
                    ps = [S[3], S[4]]
                    t3s = [softmax_row(bank[4 + c], N, A_[n][c], ps[c], None, c)[0] for c in range(2)]
                    t4 = put("dve", lambda e: e.reciprocal(RL[:, 0:2], LS[:, 0:2]), t3s)
                    smf[0], smf[1] = [t3s[0], t4], [t3s[1], t4]
                    t5 = put("dve", lambda e: e.tensor_tensor(NL, RL[:, 1:2], LAM, ALU.mult), t4, lamtok)
                    p1, p2 = ps
                    t6 = put("dve", lambda e: e.tensor_scalar(p2.ap[:, 0:N], p2.ap[:, 0:N], NL, None, ALU.mult), t5, t3s)
                    t7 = put("dve", lambda e: e.scalar_tensor_tensor(p1.ap[:, 0:N], p1.ap[:, 0:N], RL[:, 0:1], p2.ap[:, 0:N], ALU.mult, ALU.add), t6)
                    p2.free = [t7]
                    A_[n] = (p1, t7, N)

                def stage_b(n):
                    hq, i = divmod(n, 4)
                    p, tp, N = A_.pop(n)
                    b = bank[6]
                    for j in range(i + 1):
                        t = pe_transpose(b.ap[:, j * 128:(j + 1) * 128], p.ap[:, j * 128:(j + 1) * 128], ID,
                                         [tp, b.free if j == 0 else None], j == i)
                    p.free = [t]
                    j0 = 0 if i < 2 else 2
                    src = b.ap[:, 0:N].rearrange("p (j t) -> p j t", t=128)
                    cs = slice((i % 2) * 128, (i % 2) * 128 + 128)
                    ev[n] = split_scaled(src, PH[:, j0:j0 + i + 1, cs], PL[:, j0:j0 + i + 1, cs], 1.0, [t], [st["pv"], ztok])
                    b.free = ev[n]

                def stage_c(hq):
                    par = pair % 2
                    b = bank[7]
                    for a_ in range(2):
                        for j in range(2 * a_ + 2):
                            jj = (0 if a_ == 0 else 2) + j
                            t = mm3(b.ap[:, a_ * 256:a_ * 256 + 256], VV[:, 2 * par, j, hq * 128:hq * 128 + 128],
                                    VV[:, 2 * par + 1, j, hq * 128:hq * 128 + 128], PH[:, jj, :], PL[:, jj, :],
                                    [vtok[pair], ev[4 * hq + 2 * a_ + 1], ev[4 * hq + 2 * a_], b.free if j == 0 and a_ == 0 else None],
                                    j == 0, j == 2 * a_ + 1, mark=j == 2 * a_ + 1)
                    st["pv"] = t
                    return t

                def o_chain(hq, t):
                    h = 2 * pair + hq
                    b, s, x = bank[7], S[5], bank[6]
                    ts = put("act", lambda e: e.activation(s.ap, b.ap[:, :], ACT.Square), t, s.free)
                    yield
                    _, t4 = inv_rms(x, 1, 128, ts, lambda i: s.ap[:, i * 128:(i + 1) * 128], ONE, Buf(None), s.ap, 1)
                    yield
                    t5 = spread(x, Buf(None), s.ap, t4)
                    t6 = put("act", lambda e: e.activation(s.ap, x.ap[:, :], ACT.Copy), t5)
                    x.free = [t6]
                    t7 = put("dve", lambda e: e.scalar_tensor_tensor(s.ap, b.ap[:, :], SG, s.ap, ALU.mult, ALU.mult), t6)
                    b.free = [t7]
                    g_ = G[2 * (pair % 2) + hq]
                    t8 = put("dve", lambda e: e.tensor_tensor(s.ap, s.ap, g_, ALU.mult), t7, gtok[pair][hq])
                    gfree[pair % 2].append(t8)
                    r = split_scaled(s.ap, OH[:, h, :], OL[:, h, :], 1.0, [t8])
                    s.free = r
                    otok[h] = r
                    yield

                gfree[pair % 2] = []
                oc = iter(())
                for n in range(10):
                    if n < 8:
                        stage_a(n)
                        yield
                        next(oc, None)
                    if n >= 2 and (n - 2) % 4 == 3:
                        drain(oc)
                        oc = o_chain((n - 2) // 4, stage_c((n - 2) // 4))
                        next(oc)
                        yield
                    if 1 <= n <= 8:
                        stage_b(n - 1)
                    if n < 8:
                        stage_a2(n)
                    yield
                for _ in oc:
                    yield
                st["prev"] = mine

            side = chain(qk_chain(0, bank[0:2], tk[0:2], QG), qk_chain(1, bank[2:4], tk[2:4], GB[:, 26:27]))
            g2 = []
            both(tiles("dg0", bank[4:6], xk, xtok, toks=g2), side, 12)
            drain(side)
            gtok[0] = gate_evac(bank[4:6], g2, G[0:2], [], S[5])
            side = att(0)
            for t in range(1, 4):
                vt = []
                both(v_chunk(f"dv{t}", bank[0:2], xk, xtok, 4, vt), side, 4)
                vs = 2 * (t % 2)
                vtok[t] = evac_v(bank[0:2], vt, VV[:, vs], VV[:, vs + 1], 4, True, [vpv(st)])
                g2 = []
                both(tiles(f"dg{t}", bank[2:4], xk, xtok, toks=g2), side, 4)
                gtok[t] = gate_evac(bank[2:4], g2, G[2 * (t % 2):2 * (t % 2) + 2], list(gfree[t % 2]), S[2])
                tq = []
                both(tiles(f"dq{t}", bank[0:2], xk, xtok, toks=tq), side, 4)
                drain(side)
                c1 = qk_chain(0, bank[0:2], tq, QG)
                tk2 = []
                both(tiles(f"dk{t}", bank[2:4], xk, xtok, toks=tk2), c1, 7)
                drain(c1)
                c2 = qk_chain(1, bank[2:4], tk2, GB[:, 26:27])
                side = chain(c2, att(t))
            rb.free = q.now()

            def ok(k):
                return OH[:, k, :], OL[:, k, :]

            for _ in range(16):
                next(side)
            out_proj("d", ok, otok, gnext, side)

        def vpv(st):
            return st["pv"]

        def x_norm2_a():
            x_norm_b()
            tr = rbt["rb"]
            for m in range(KT):
                g_ = GA[:, 96 + m:97 + m]
                tx = put("dve", lambda e, m=m, g_=g_: e.scalar_tensor_tensor(X[:, m, :], X[:, m, :], g_, RB[:, :], ALU.mult, ALU.mult), tr, xtok[m])
                square_x(m, tx)

        def x_norm2_b():
            r1 = RL
            t = put("dve", lambda e: e.tensor_copy(LT[:, 0:4], RCOL), rbt["rcol"])
            acc = S[5]
            pwfree["rcol"] = [t]
            for i in range(4):
                tt = mm(bank[6].ap[:, i:i + 1], acc.ap[:, i * 128:(i + 1) * 128], ONE, [accx["tok"], bank[6].free if i == 0 else None], mark=i == 3)
            acc.free = [tt]
            t1 = put("dve", lambda e: e.tensor_scalar(MS[:, 0:4], bank[6].ap[:, 0:4], 1.0 / D, EPS, ALU.mult, ALU.add), tt, pwfree["ms"])
            bank[6].free = [t1]
            t2 = put("pool", lambda e: e.tensor_tensor(PW[:, 0:4], MS[:, 0:4], NH[:, 0:4], ALU.pow), t1, pwfree["pw"])
            pwfree["ms"] = [t2]
            t3 = put("dve", lambda e: e.tensor_tensor(RCOL, PW[:, 0:4], LT[:, 0:4], ALU.mult), t2, t, q.now()[2])
            pwfree["pw"] = [t3]
            rbt["rcol"] = t3
            s = S[4]
            t4 = put("dve", lambda e: e.tensor_copy(s.ap.rearrange("p (i w) -> p i w", i=4), RCOL.unsqueeze(2).to_broadcast([128, 4, 128])), t3, s.free)
            rb.free = q.now()
            t5 = spread(bank[6], s, s.ap, t4)
            t6 = put("act", lambda e: e.activation(RB[:, :], bank[6].ap[:, :], ACT.Copy), t5, rb.free)
            bank[6].free = [t6]
            rbt["rb"] = t6

        def plan_sb():
            wkv, w, wo = a["w_kv_2"], a["b_w_in_2"][0], a["b_w_out_2"][0]
            gk, gb = 112, 120
            plan_cols("sq0", w, 0, gain=gb)
            plan_cols("sk0", wkv, 0, gain=gk)
            plan_cols("sv0", wkv, D, gain=gk)
            plan_cols("sg0", w, D, gain=gb)
            for t in range(1, 4):
                plan_cols(f"sv{t}", wkv, D + t * 256, gain=gk)
                plan_cols(f"sg{t}", w, D + t * 256, gain=gb)
                plan_cols(f"sq{t}", w, t * 256, gain=gb)
                plan_cols(f"sk{t}", wkv, t * 256, gain=gk)
            for p in range(4):
                plan_cols(f"so{p}", wo, p * 256)

        def stick(snap):
            OH = AR[:, 0:4096].rearrange("p (k t) -> p k t", t=T)
            OL = AR[:, 4096:8192].rearrange("p (k t) -> p k t", t=T)
            QK = AR[:, 8192:12288].rearrange("p (k t) -> p k t", t=T)
            QH, QL, KH, KL = QK[:, 0:2], QK[:, 2:4], QK[:, 4:6], QK[:, 6:8]
            VV = AR[:, 12288:16384].rearrange("p (s i c) -> p s i c", s=4, c=256)
            LO = [[0, 512, 896, 1152], [0, 512, 896, 1280]]
            LH, LL = AR[:, 16384:17792], AR[:, 17792:19200]
            EH = [AR[:, 19200 + i * T:19200 + (i + 1) * T] for i in range(2)]
            EL = [AR[:, 20224 + i * T:20224 + (i + 1) * T] for i in range(2)]
            TRI = AR[:, 21248:21376]
            NEG = AR[:, 21376:21504]
            G = [AF[:, i * T:i * T + T] for i in range(4)]
            TMP = AF[:, 2048:2304]
            tk = [None] * 4
            drain(two_chunks("sq0", "sk0", bank[0:4], xk, xtok, tk))
            x_norm_a()
            vt = []
            g = v_chunk("sv0", bank[4:6], xk, xtok, 4, vt)
            next(g)
            x_norm_b()
            drain(g)
            barrier(snap)
            MR = AR[:, 21504:21632]
            ct = [shape_matrix(MR, C_MK, snap), shape_matrix(TRI, C_TRI, snap)]
            c2 = put("dve", lambda e: e.memset(TMP[:, 0:128], -1.0))
            ct.append(put("act", lambda e: e.activation(NEG, TMP[:, 0:128], ACT.Copy), c2))
            qkt = [evac_rb(bank[i], tk[i], S[i % 2], (QH, KH)[i // 2][:, i % 2, :], (QL, KL)[i // 2][:, i % 2, :],
                           0.125 if i < 2 else 1.0) for i in range(4)]
            vtok, gtok = [None] * 4, [None] * 4
            vtok[0] = evac_v(bank[4:6], vt, VV[:, 0], VV[:, 1], 4, True, ())
            otok = [None] * 8
            st = {"prev": [], "pv": None, "lr": [None] * 5, "er": [[], []]}
            gfree = [[], []]

            def att(quad):
                mine = []
                par = quad % 2
                gfree[par] = []
                Z, E_ = {}, {}
                lt = {}

                def stage_a(n):
                    hq, jr = divmod(n, 4)
                    j = 3 - jr
                    tl, hh = divmod(hq, 2)
                    r = slice(64 * hh, 64 * hh + 64)
                    N = T - 128 * j
                    b = bank[4 + n % 3]
                    o = b.ap[:, 0:N]
                    ks = slice(j * 128, j * 128 + 128)
                    qs = slice(j * 128, T)
                    t = mm3(o, KH[r, tl, ks], KL[r, tl, ks], QH[r, tl, qs], QL[r, tl, qs], [qkt[tl], qkt[2 + tl], b.free], True, True, mark=True)
                    mine.append(t)
                    s = S[2 + n % 2]
                    x = s.ap[:, 0:N]
                    t1 = put("act", lambda e: e.activation(x, o, ACT.Abs), t, s.free)
                    t1 = put("act", lambda e: e.activation(x, x, ACT.Exp, scale=-1.0), t1)
                    t1 = put("act", lambda e: e.activation(x, x, ACT.Ln, bias=1.0), t1)
                    t2 = put("dve", lambda e: e.scalar_tensor_tensor(x, o, 0.0, x, ALU.max, ALU.add), t1)
                    t3 = put("pool", lambda e: e.affine_select(out=x[:, 0:128], in_=x[:, 0:128], compare_op=ALU.is_gt, fill=0.0,
                                                               base=0, pattern=[[1, 128]], channel_multiplier=-1), t2)
                    lo = LO[hq % 2][j]
                    lh, ll = LH[:, lo:lo + N], LL[:, lo:lo + N]
                    t4 = put("dve", lambda e: e.tensor_copy(lh, x), t2, t3, st["lr"][j if j < 3 else 3 + hq % 2])
                    t5 = put("dve", lambda e: e.tensor_tensor(ll, x, F(lh), ALU.subtract), t4, t3)
                    s.free = [t5]
                    lt[n] = [t4, t5]
                    Z[n] = (b, o, N, j)

                def stage_b(n):
                    hq, jr = divmod(n, 4)
                    b, o, N, j = Z.pop(n)
                    for j2 in range(j, 4):
                        n2 = 4 * hq + 3 - j2
                        m = T - 128 * j2
                        dst = b.ap[:, (j2 - j) * 128:(j2 - j) * 128 + m]
                        w_ = TRI if j2 == j else NEG
                        lo = LO[hq % 2][j2]
                        mm(dst, w_, LH[:, lo:lo + m], [lt[n2], ct], False, False, False, True)
                        t = mm(dst, w_, LL[:, lo:lo + m], (), False, False, True, True)
                        if j == 0:
                            st["lr"][j2 if j2 < 3 else 3 + hq % 2] = t
                    t = mm(b.ap[:, 0:128], IDR[:, :], MR, [ct], False, True, True, True)
                    s = S[4 + n % 2]
                    x = s.ap[:, 0:N]
                    t1 = put("act", lambda e: e.activation(x, o, ACT.Exp), t, s.free)
                    b.free = [t1]
                    eh, el = EH[n % 2][:, 0:N], EL[n % 2][:, 0:N]
                    t2 = put("dve", lambda e: e.tensor_copy(eh, x), t1, st["er"][n % 2])
                    t3 = put("dve", lambda e: e.tensor_tensor(el, x, F(eh), ALU.subtract), t2)
                    s.free = [t3]
                    E_[n] = (N, j, [t2, t3])

                def stage_c(n):
                    hq, jr = divmod(n, 4)
                    tl, hh = divmod(hq, 2)
                    N, j, te = E_.pop(n)
                    b = bank[7]
                    vs = VV[:, 2 * par, j, tl * 128:tl * 128 + 128], VV[:, 2 * par + 1, j, tl * 128:tl * 128 + 128]
                    t = mm3(b.ap[:, j * 128:T], vs[0], vs[1], EH[n % 2][:, 0:N], EL[n % 2][:, 0:N],
                            [te, vtok[quad], b.free if jr == 0 else None], jr == 0, jr == 3, mark=True, skip=True)
                    st["er"][n % 2] = [t]
                    if jr == 3:
                        st["pv"] = t
                        r = slice(64 * hh, 64 * hh + 64)
                        g_ = G[2 * par + tl][r, :]
                        t1 = put("dve", lambda e: e.scalar_tensor_tensor(g_, b.ap[r, :], 0.5, g_, ALU.mult, ALU.mult), t, gtok[quad])
                        b.free = [t1]
                        kt = 2 * quad + tl
                        rr = split_scaled(g_, OH[r, kt, :], OL[r, kt, :], 1.0, [t1])
                        gfree[par].append(rr)
                        otok[kt] = [otok[kt], rr]

                for n in range(18):
                    if n < 16:
                        stage_a(n)
                        yield
                    if 1 <= n <= 16:
                        stage_b(n - 1)
                        yield
                    if n >= 2:
                        stage_c(n - 2)
                        yield
                st["prev"] = mine

            g2 = []
            drain(tiles("sg0", bank[0:2], xk, xtok, toks=g2))
            gtok[0] = gate_evac(bank[0:2], g2, G[0:2], [], S[2])
            put("act", lambda e: e.preload_act_table_set("natural_log_exp_and_others"), mark=False)
            side = att(0)
            for t in range(1, 4):
                vt = []
                both(v_chunk(f"sv{t}", bank[0:2], xk, xtok, 4, vt), side, 4)
                vs = 2 * (t % 2)
                vtok[t] = evac_v(bank[0:2], vt, VV[:, vs], VV[:, vs + 1], 4, True, [vpv(st)])
                g2 = []
                both(tiles(f"sg{t}", bank[2:4], xk, xtok, toks=g2), side, 8)
                tq, tk2 = [], []
                both(tiles(f"sq{t}", bank[0:2], xk, xtok, toks=tq), side, 8)
                drain(side)
                gtok[t] = gate_evac(bank[2:4], g2, G[2 * (t % 2):2 * (t % 2) + 2], list(gfree[t % 2]), S[2])
                put("act", lambda e: e.preload_act_table_set("natural_log_exp_and_others"), mark=False)
                for j in range(2):
                    qkt[j] = evac_rb(bank[j], tq[j], S[j], QH[:, j, :], QL[:, j, :], 0.125, st["prev"])
                drain(tiles(f"sk{t}", bank[2:4], xk, xtok, toks=tk2))
                for j in range(2):
                    qkt[2 + j] = evac_rb(bank[2 + j], tk2[j], S[j], KH[:, j, :], KL[:, j, :], 1.0, st["prev"])
                side = att(t)

            def ok(k):
                return OH[:, k, :], OL[:, k, :]

            out_proj("s", ok, otok, None, side, fin=True)

        GOFF = {"g_ffn1": 0, "g_mix": 16, "g_xattn": 32, "g_mem": 48, "g_ffn2": 64}

        for r in range(4):
            plan(("x", r), a["x"][0, r * 128:(r + 1) * 128, :].rearrange("p (k c) -> p k c", c=128), kind="raw")
        seq = list(stages)
        for sname in seq:
            nm, _, l = sname.partition("_")
            if nm in ("ffn1", "ffn2"):
                plan_ffn(sname, a[f"w_{nm}_gu"][int(l)], a[f"w_{nm}_down"][int(l)])
            elif nm == "mix":
                plan_mix(int(l))
                at = len(units) - 4
                if f"x_{l}" in seq:
                    for r in range(2):
                        units.insert(at + r, ((f"mem{l}", r), a["mem"][0, r * 128:(r + 1) * 128, :].rearrange("p (k c) -> p k c", c=128), None, "raw"))
            elif nm == "x":
                plan_x(int(l))
            elif nm == "diff":
                plan_diff()
            else:
                plan_sb()

        tmp = AF[:, 0:256]
        d0 = put("sp", lambda e: e.dma_start(tmp, consts[:, C_ID:C_ID + 256]), sem="c0", by=16)
        d1 = put("sp", lambda e: e.dma_start(BLK, consts[:, C_BLK:C_BLK + 2]), sem="c1", by=16)
        ga, gb = AF[:, 256:384], AF[:, 384:512]
        gt = []
        zt = put("dve", lambda e: e.memset(AF[:, 256:512], 0.0))
        dn = 0

        def grow(dst, src):
            nonlocal dn
            gt.append(put("sp", lambda e: e.dma_start(dst, src), zt, sem=f"g{dn}", by=16))
            dn += 1

        for nm in ("g_ffn1", "g_mix", "g_xattn", "g_mem", "g_ffn2"):
            o = GOFF[nm]
            grow(ga[o:o + 16, :], a[nm].rearrange("l (k p) -> (l k) p", p=128))
        grow(ga[80:88, :], a["g_conv_out"].rearrange("l (k p) -> (l k) p", p=128))
        grow(ga[88:96, :], a["g_att_out"].rearrange("l (k p) -> (l k) p", p=128))
        grow(ga[96:104, :], a["g_final"].rearrange("(k p) -> k p", p=128))
        grow(ga[104:112, :], a["a_norm_2"].rearrange("l (k p) -> (l k) p", p=128))
        grow(ga[112:120, :], a["kv_norm_2"].rearrange("(k p) -> k p", p=128))
        grow(ga[120:128, :], a["b_norm_2"].rearrange("l (k p) -> (l k) p", p=128))
        grow(gb[0:24, :], a["w_conv"].rearrange("l k (m p) -> (l k m) p", p=128))
        grow(gb[24:25, :], a["a_subln_2"])
        for c in range(2):
            grow(gb[25:26, c * 64:c * 64 + 64], a["a_q_norm_2"])
            grow(gb[26:27, c * 64:c * 64 + 64], a["a_k_norm_2"])
        for i, nm in enumerate(("a_lq1_2", "a_lk1_2", "a_lq2_2", "a_lk2_2")):
            grow(AF[0:1, 512 + 64 * i:576 + 64 * i], a[nm])
        for l in range(2):
            grow(BF[0:8, l:l + 1], a["b_f"][l].rearrange("(p o) -> p o", o=1))
        k1 = put("act", lambda e: e.activation(IDR[:, :], tmp[:, 0:128], ACT.Copy), d0)
        k3 = put("dve", lambda e: e.memset(ONE, 1.0))
        k4 = put("dve", lambda e: e.memset(NH, -0.5))
        pe_transpose(bank[7].ap[:, 0:128], ga, ID, [k1, gt], False)
        t = pe_transpose(bank[7].ap[:, 128:256], gb, ID, (), True)
        t1 = put("dve", lambda e: e.tensor_copy(GA[:, :], bank[7].ap[:, 0:128]), t)
        t2 = put("dve", lambda e: e.tensor_copy(GB[:, :], bank[7].ap[:, 128:160]), t)
        t3 = put("dve", lambda e: e.tensor_scalar(QG, GB[:, 25:26], 0.125, None, ALU.mult), t2)
        t4 = put("dve", lambda e: e.tensor_scalar(SG, GB[:, 24:25], 0.5 * (1.0 - LAMBDA_INIT), None, ALU.mult), t2)
        t5 = put("dve", lambda e: e.tensor_tensor(GG, GA[:, 96:104], GA[:, 104:112], ALU.mult), t1)
        lr = AF[0:1, 512:768]
        u1 = put("dve", lambda e: e.tensor_tensor(AF[0:1, 768:832], lr[:, 0:64], lr[:, 64:128], ALU.mult), gt)
        u2 = put("dve", lambda e: e.tensor_tensor(AF[0:1, 832:896], lr[:, 128:192], lr[:, 192:256], ALU.mult), gt)
        u3 = put("dve", lambda e: e.reduce_sum(LT[0:1, 0:2], AF[0:1, 768:896].rearrange("p (a c) -> p a c", a=2), AX), u1, u2)
        u4 = put("act", lambda e: e.activation(LT[0:1, 2:4], LT[0:1, 0:2], ACT.Exp), u3)
        u5 = put("dve", lambda e: e.tensor_tensor(LT[0:1, 0:1], LT[0:1, 3:4], LT[0:1, 2:3], ALU.subtract), u4, u3)
        u5 = put("dve", lambda e: e.tensor_scalar(LT[0:1, 0:1], LT[0:1, 0:1], -LAMBDA_INIT, None, ALU.add), u5)
        u6 = put("dve", lambda e: e.memset(AF[0:1, 896:1024], 1.0))
        u7 = mm(bank[7].ap[:, 256:257], AF[0:1, 896:1024], LT[0:1, 0:1], [u5, u6, t1, t2])
        lamtok = put("dve", lambda e: e.tensor_copy(LAM, bank[7].ap[:, 256:257]), u7)
        bank[7].free = [lamtok]
        start = [k1, k3, k4, t1, t2, t3, t4, t5, lamtok, d1, gt]
        for e in ("pe", "act", "dve", "pool"):
            q.hold(e, start)

        def gains(i):
            if i >= len(seq):
                return None
            nm, _, l = seq[i].partition("_")
            if nm == "diff":
                return lambda m: GG[:, m:m + 1]
            if nm == "sb":
                return None
            base = {"ffn1": 0, "mix": 16, "x": 32, "ffn2": 64}[nm]
            return gc(base + 8 * int(l))

        us = [get(("x", r)) for r in range(3)]
        g0 = gains(0)
        xt = []
        for i in range(4):
            if i == 3:
                us.append(get(("x", 3)))
            row = us[i][0].rearrange("p k c -> p (k c)")
            for hf in range(2):
                b = bank[2 * (i % 2) + hf]
                for j in range(4):
                    k = 4 * hf + j
                    t = pe_transpose(b.ap[:, j * 128:(j + 1) * 128], row[:, k * 128:(k + 1) * 128], ID,
                                     [us[i][1], b.free if j == 0 else None], j == 3)
                dst = X[:, 4 * hf:4 * hf + 4, i * 128:(i + 1) * 128]
                src = b.ap[:, :].rearrange("p (j t) -> p j t", t=128)
                if hf:
                    t2 = put("act", lambda e, dst=dst, src=src: e.activation(dst, src, ACT.Copy), t)
                else:
                    t2 = put("dve", lambda e, dst=dst, src=src: e.tensor_copy(dst, src), t)
                b.free = [t2]
                xt.append(t2)
            raw_done(us[i], [t])
            pump()
        for m in range(KT):
            x_post(m, xt, g0)

        snap = q.now()
        for i, sname in enumerate(seq):
            nm, _, l = sname.partition("_")
            nxt = gains(i + 1)
            if nm in ("ffn1", "ffn2"):
                ffn(sname, snap, nxt)
            elif nm == "mix":
                ms = mem_prep(int(l), 48 + 8 * int(l)) if f"x_{l}" in seq else iter(())
                mix(int(l), snap, nxt, ms)
            elif nm == "x":
                xattn(int(l), snap, nxt)
            elif nm == "diff":
                diff(snap, nxt)
            else:
                stick(snap)
            snap = q.now()
            rb.free = snap
            pwfree["rcol"] = snap
        store(snap)

        sems = {s: ctx.enter_context(nc.semaphore(f"s_{s}")) for s in q.count}
        block = ctx.enter_context(nc.Block())

        @block.tensor
        def _(e):
            q.run("pe", e, sems)

        @block.scalar
        def _(e):
            q.run("act", e, sems)

        @block.vector
        def _(e):
            q.run("dve", e, sems)

        @block.gpsimd
        def _(e):
            q.run("pool", e, sems)

        @block.sync
        def _(e):
            with nc.allow_non_contiguous_dma(reason="eight gate columns and biases"):
                q.run("sp", e, sems)


_INS = ["x", "mem", "g_ffn1", "w_ffn1_gu", "w_ffn1_down", "g_mix", "w_mix_in", "w_conv", "b_f", "g_conv_out", "g_att_out",
        "w_mix_out", "g_xattn", "g_mem", "w_xq", "w_xkv", "w_xo", "g_ffn2", "w_ffn2_gu", "w_ffn2_down", "g_final",
        "a_norm_2", "a_w_in_2", "a_w_out_2", "a_q_norm_2", "a_k_norm_2", "a_lq1_2", "a_lk1_2", "a_lq2_2", "a_lk2_2",
        "a_subln_2", "kv_norm_2", "w_kv_2", "b_norm_2", "b_w_in_2", "b_w_out_2"]


def kernel(**inputs):
    import numpy as _np
    import concourse.bacc as _bacc
    from concourse import mybir as _mybir
    from concourse.bass_utils import run_bass_kernel_spmd as _run

    nc = _bacc.Bacc("TRN2", target_bir_lowering=False, num_devices=1)
    arrays, args = {}, {}
    for name in _INS:
        v = _np.ascontiguousarray(inputs[name])
        arrays[f"in_{name}_dram"] = v
        args[name] = nc.dram_tensor(f"in_{name}_dram", v.shape, _mybir.dt.from_np(v.dtype), kind="ExternalInput").ap()
    c = shape_constants()
    arrays["in_consts_dram"] = c
    cd = nc.dram_tensor("in_consts_dram", c.shape, _mybir.dt.float32, kind="ExternalInput").ap()
    out = nc.dram_tensor("out_0_dram", (1, T, D), _mybir.dt.float32, kind="ExternalOutput").ap()
    program(nc, args, cd, out, STAGES)
    r = _run(nc, [arrays], core_ids=[0])
    return r.results[0]["out_0_dram"]
```

```python
from contextlib import ExitStack

import numpy as np

import concourse.bass as bass
from concourse import mybir

F32 = mybir.dt.float32
F32R = mybir.dt.float32r
ALU = mybir.AluOpType
ACT = mybir.ActivationFunctionType
AX = mybir.AxisListType.X

T = 512
D = 1024
KT = 8
FF = 2816
NF = FF // 128
CW = 512
EPS = 1e-6
BIG = -1.0e30
LAMBDA_INIT = 0.8 - 0.6 * float(np.exp(0.0))
NSLOT = 4
NRAW = 3
NS = 6
STAGES = ["ffn1_0", "mix_0", "x_0", "ffn2_0", "ffn1_1", "mix_1", "x_1", "ffn2_1", "diff", "sb"]

C_ID, C_MQ, C_MK, C_TRI, C_ROT, C_COS, C_SIN, C_BLK, C_N = 0, 128, 256, 384, 512, 640, 1152, 1664, 1666


def shape_constants():
    c = np.zeros((128, C_N), np.float32)
    a = np.arange(128)
    c[:, C_ID:C_ID + 128] = np.eye(128)
    c[:, C_MQ:C_MQ + 128] = np.where(a[None, :] > a[:, None], BIG, 0.0)
    c[:, C_MK:C_MK + 128] = np.where(a[None, :] <= a[:, None], BIG, 0.0)
    c[:, C_TRI:C_TRI + 128] = np.where(a[:, None] >= a[None, :], -1.0, 0.0)
    half = 8
    inv = np.power(np.float32(500000.0), -np.arange(half, dtype=np.float32) / np.float32(half)).astype(np.float32)
    ang = (np.arange(T, dtype=np.float32)[:, None] * inv[None, :]).astype(np.float32)
    cos, sin = np.cos(ang).T, np.sin(ang).T
    c[:, C_COS:C_COS + T] = 1.0
    for b in (0, 64):
        for j in range(half):
            c[b + j, C_COS:C_COS + T] = cos[j]
            c[b + half + j, C_COS:C_COS + T] = cos[j]
            c[b + j, C_SIN:C_SIN + T] = -sin[j]
            c[b + half + j, C_SIN:C_SIN + T] = sin[j]
            c[b + half + j, C_ROT + b + j] = 1.0
            c[b + j, C_ROT + b + half + j] = 1.0
    c[0:64, C_BLK] = 1.0
    c[64:128, C_BLK + 1] = 1.0
    return c


class Later:

    def activation(self, *a, **k):
        return lambda e: e.activation(*a, **k)

    def affine_select(self, *a, **k):
        return lambda e: e.affine_select(*a, **k)

    def dma_start(self, *a, **k):
        return lambda e: e.dma_start(*a, **k)

    def matmul(self, *a, **k):
        return lambda e: e.matmul(*a, **k)

    def memset(self, *a, **k):
        return lambda e: e.memset(*a, **k)

    def preload_act_table_set(self, *a, **k):
        return lambda e: e.preload_act_table_set(*a, **k)

    def reciprocal(self, *a, **k):
        return lambda e: e.reciprocal(*a, **k)

    def reduce_max(self, *a, **k):
        return lambda e: e.reduce_max(*a, **k)

    def reduce_sum(self, *a, **k):
        return lambda e: e.reduce_sum(*a, **k)

    def scalar_tensor_tensor(self, *a, **k):
        return lambda e: e.scalar_tensor_tensor(*a, **k)

    def tensor_copy(self, *a, **k):
        return lambda e: e.tensor_copy(*a, **k)

    def tensor_scalar(self, *a, **k):
        return lambda e: e.tensor_scalar(*a, **k)

    def tensor_tensor(self, *a, **k):
        return lambda e: e.tensor_tensor(*a, **k)

    def tensor_tensor_scan(self, *a, **k):
        return lambda e: e.tensor_tensor_scan(*a, **k)

    def transpose(self, *a, **k):
        return lambda e: e.transpose(*a, **k)


LATER = Later()


class Queues:

    def __init__(self):
        self.items = {e: [] for e in ("pe", "act", "dve", "pool", "sp")}
        self.count = {}
        self.met = {e: {} for e in self.items}

    def put(self, eng, fn, *waits, sem=None, by=1, mark=True):
        need = {}
        if eng == "pool" and self.count.get("pool"):
            waits = (waits, ("pool", self.count["pool"]))
        for w in flat(waits):
            need[w[0]] = max(need.get(w[0], 0), w[1])
        met = self.met[eng]
        ws = [(s, v) for s, v in need.items() if met.get(s, 0) < v]
        met.update(ws)
        sem = sem or eng
        if mark:
            self.count[sem] = self.count.get(sem, 0) + by
        self.items[eng].append((ws, fn and fn(LATER), (sem, by) if mark else None))
        return (sem, self.count[sem]) if mark else None

    def now(self):
        return [(e, self.count.get(e, 0)) for e in ("pe", "act", "dve", "pool")]

    def hold(self, eng, waits):
        self.put(eng, None, waits, mark=False)

    def run(self, eng, e, sems):
        for ws, fn, inc in self.items[eng]:
            for s, v in ws:
                e.wait_ge(sems[s], v)
            if fn is not None:
                ins = fn(e)
                if inc:
                    ins.then_inc(sems[inc[0]], inc[1])


def flat(w):
    if w is None:
        return
    if isinstance(w, tuple) and len(w) == 2 and isinstance(w[0], str):
        yield w
        return
    for x in w:
        yield from flat(x)


class Buf:

    def __init__(self, ap):
        self.ap = ap
        self.free = []


def program(nc, a, consts, out, stages):
    q = Queues()
    put = q.put
    ctx = ExitStack()
    with ctx:
        def sb(name, shape, dt=F32):
            return ctx.enter_context(nc.sbuf_tensor(name, shape, dt))

        X = sb("X", [128, KT, T])
        XH = sb("XH", [128, KT, T], F32R)
        XL = sb("XL", [128, KT, T], F32R)
        RAW = sb("RAW", [128, NRAW, 1024])
        WH = sb("WH", [128, NSLOT, 1024], F32R)
        WL = sb("WL", [128, NSLOT, 1024], F32R)
        AR = sb("AR", [128, 88 * 256], F32R)
        AF = sb("AF", [128, 3108])
        SC = sb("SC", [128, NS, T])
        RB = sb("RB", [128, T])
        IDR = sb("IDR", [128, 128], F32R)
        ID = IDR[:, :].bitcast(F32)
        GA = sb("GA", [128, 128])
        GB = sb("GB", [128, 32])
        SM = sb("SM", [128, 80])
        PS = [ctx.enter_context(nc.psum_tensor(f"PS{i}", [128, 512], F32)) for i in range(8)]
        bank = [Buf(p) for p in PS]
        S = [Buf(SC[:, i, :]) for i in range(NS)]

        ONE = SM[:, 0:1]
        BLK = SM[:, 1:3]
        NH = SM[:, 3:11]
        RCOL = SM[:, 11:15]
        MS = SM[:, 15:23]
        PW = SM[:, 23:31]
        MX = SM[:, 31:33]
        NB = SM[:, 33:35]
        LS = SM[:, 35:37]
        RL = SM[:, 37:39]
        MSS = SM[:, 39:43]
        GG = SM[:, 43:51]
        LAM = SM[:, 51:52]
        QG = SM[:, 52:53]
        SG = SM[:, 53:54]
        BF = SM[:, 54:56]
        LT = SM[:, 56:60]
        NL = SM[:, 60:61]

        def F(ap):
            return ap.bitcast(F32)

        names = set()

        units = []

        def plan(key, ap, gain=None, kind="w"):
            units.append((key, ap, gain, kind))

        def plan_cols(name, w, c0, cols=256, gain=None, nk=KT):
            for u in range(0, nk, 4):
                n = min(4, nk - u)
                src = w[u * 128:(u + n) * 128, c0:c0 + cols].rearrange("(k p) c -> p k c", p=128)
                plan((name, u // 4), src, None if gain is None else (gain, u))

        def plan_two(n0, w0, c0, n1, w1, c1, g0=None, g1=None):
            at = len(units)
            plan_cols(n0, w0, c0, gain=g0)
            plan_cols(n1, w1, c1, gain=g1)
            a0, a1, b0, b1 = units[at:]
            units[at:] = [a0, b0, a1, b1]

        raws = [Buf(RAW[:, i, :]) for i in range(NRAW)]
        slots = [Buf(None) for _ in range(NSLOT)]
        state = {"dma": 0, "split": 0, "slotseq": 0, "upto": 0}
        loaded = {}
        ready = {}
        held = [False] * NSLOT
        rawheld = [False] * NRAW

        def pump():
            while True:
                moved = False
                n = state["dma"]
                if n < len(units) and not rawheld[n % NRAW]:
                    key, ap, gain, kind = units[n]
                    r = raws[n % NRAW]
                    sh = ap.shape
                    dst = r.ap[:, 0:sh[1] * sh[2]].rearrange("p (k c) -> p k c", c=sh[2])
                    tok = put("sp", lambda e, d=dst, s=ap: e.dma_start(d, s), r.free, sem=f"raw{n % NRAW}", by=16)
                    loaded[n] = (tok, dst)
                    rawheld[n % NRAW] = True
                    state["dma"] += 1
                    moved = True
                m = state["split"]
                if m < state["dma"]:
                    key, ap, gain, kind = units[m]
                    tok, dst = loaded[m]
                    if kind == "raw":
                        ready[key] = (dst, tok, m)
                        state["split"] += 1
                        moved = True
                    elif m < state["upto"] and not held[state["slotseq"] % NSLOT]:
                        s = state["slotseq"] % NSLOT
                        state["slotseq"] += 1
                        held[s] = True
                        nk, ncol = ap.shape[1], ap.shape[2]
                        pc = 128 if kind == "pad" else ncol
                        h = WH[:, s, 0:nk * pc].rearrange("p (k c) -> p k c", c=pc)
                        l = WL[:, s, 0:nk * pc].rearrange("p (k c) -> p k c", c=pc)
                        fr = slots[s].free
                        if kind == "pad":
                            z1 = put("pool", lambda e, h=h: e.memset(F(h), 0.0), fr)
                            z2 = put("pool", lambda e, l=l: e.memset(F(l), 0.0), fr)
                            fr = [z1, z2]
                        hd, ld = h[:, :, 0:ncol], l[:, :, 0:ncol]
                        if gain is None:
                            t1 = put("act", lambda e, o=hd, i=dst: e.activation(o, i, ACT.Copy), tok, fr)
                            t2 = put("dve" if key[0].startswith("ffn") else "pool",
                                     lambda e, o=ld, i=dst, h=hd: e.tensor_tensor(o, i, F(h), ALU.subtract), t1, fr, tok)
                        else:
                            g0, ku = gain
                            for k in range(nk):
                                gc = GA[:, g0 + ku + k:g0 + ku + k + 1]
                                t1 = put("act", lambda e, o=hd[:, k, :], i=dst[:, k, :], g=gc: e.activation(o, i, ACT.Copy, scale=g), tok, fr)
                                t2 = put("dve", lambda e, o=ld[:, k, :], i=dst[:, k, :], h=hd[:, k, :], g=gc:
                                         e.scalar_tensor_tensor(o, i, g, F(h), ALU.mult, ALU.subtract), t1, fr)
                        raws[m % NRAW].free = [t1, t2]
                        rawheld[m % NRAW] = False
                        ready[key] = (h, l, [t1, t2], s)
                        state["split"] += 1
                        moved = True
                if not moved:
                    return

        def get(key):
            pump()
            assert key in ready, (key, units[state["split"]][0] if state["split"] < len(units) else None)
            return ready.pop(key)

        def done(u, tok):
            slots[u[3]].free = [tok]
            held[u[3]] = False

        def raw_done(u, toks):
            raws[u[2] % NRAW].free = toks
            rawheld[u[2] % NRAW] = False

        def mm(o, l, r, waits=(), start=True, stop=True, mark=True, skip=False):
            return put("pe", lambda e: e.matmul(o, l, r, start=start, stop=stop, skip_group_check=skip), waits, mark=mark)

        def mm3(o, lh, ll, rh, rl, waits, start, stop, mark=False, skip=False):
            mm(o, ll, rh, waits, start, False, False, skip)
            mm(o, lh, rl, (), False, False, False, skip)
            return mm(o, lh, rh, (), False, stop, mark, skip)

        def pe_transpose(o, i, idn, waits, mark):
            return put("pe", lambda e: e.transpose(o, i, idn), waits, mark=mark)

        xtok = [None] * KT

        def xk(k):
            return XH[:, k, :], XL[:, k, :]

        def tiles(name, banks, rhs, rtok, ks=None, toks=None, cols=2, nu=2, n=T, part=None):
            us = []
            for u in range(nu):
                w = get((name, u))
                nk = w[0].shape[1]
                for k in range(nk):
                    kk = 4 * u + k
                    rh, rl = rhs(kk)
                    last = u == nu - 1 and k == nk - 1
                    for c in range(cols):
                        b = banks[c]
                        t = mm3(b.ap[:, 0:n], w[0][:, k, c * 128:(c + 1) * 128], w[1][:, k, c * 128:(c + 1) * 128],
                                rh, rl, [w[2] if k == 0 and c == 0 else None, rtok[kk] if c == 0 else None,
                                         b.free if kk == 0 else None],
                                kk == 0, last, mark=last or (k == nk - 1 and c == cols - 1))
                        if last:
                            us.append(t)
                        if not (k == nk - 1 and c == cols - 1):
                            yield n // 256
                done(w, t)
                pump()
                if u == nu - 1:
                    toks.extend(us)
                yield n // 256

        def two_chunks(n0, n1, banks, rhs, rtok, toks):
            ws = [get((n0, 0)), None, get((n1, 0)), None]

            def part(j, ks, fin):
                ch, u = divmod(j, 2)
                w = ws[j]
                for k in ks:
                    kk = 4 * u + k
                    rh, rl = rhs(kk)
                    for c in range(2):
                        b = banks[2 * ch + c]
                        t = mm3(b.ap[:, :], w[0][:, k, c * 128:(c + 1) * 128], w[1][:, k, c * 128:(c + 1) * 128],
                                rh, rl, [w[2], rtok[kk], b.free if kk == 0 else None], kk == 0, kk == 7,
                                mark=kk == 7 or (k == ks[-1] and c == 1))
                        if kk == 7:
                            toks[2 * ch + c] = t
                        yield 2
                if fin:
                    done(w, t)
                    pump()

            yield from part(0, range(4), True)
            ws[1] = get((n0, 1))
            yield from part(2, range(4), True)
            ws[3] = get((n1, 1))
            yield from part(1, (0, 1), False)
            yield from part(3, (0, 1), False)
            yield 0
            yield from part(1, (2, 3), True)
            yield from part(3, (2, 3), True)

        def drain(g):
            for _ in g:
                pass

        def weave(main, *sides):
            for n in main:
                for sd in sides:
                    sd[2] += n * sd[1]
                    while sd[2] >= 1:
                        sd[2] -= 1
                        next(sd[0], None)

        def stream(g, rate):
            return [g, rate, 0.0]

        def finish(sd):
            for _ in sd[0]:
                pass

        def pause(n):
            for _ in range(n):
                yield

        def chain(*gs):
            for g in gs:
                yield from g

        rb = Buf(RB[:, :])
        rbt = {"rb": None, "rcol": None}

        def inv_rms(bk, n, width, waits_pe, lhs, rhs, r4, r4ap, groups, mark_rcol=None, ms=MS, pw=PW):
            for i in range(4):
                t = mm(bk.ap[:, i * groups:(i + 1) * groups], lhs(i), rhs, [waits_pe, bk.free if i == 0 else None], mark=i == 3)
            m = 4 * groups
            t1 = put("dve", lambda e: e.tensor_scalar(ms[:, 0:m], bk.ap[:, 0:m], 1.0 / width, EPS, ALU.mult, ALU.add),
                     t, pwfree["ms"])
            bk.free = [t1]
            dst = mark_rcol if mark_rcol is not None else pw[:, 0:m]
            t2 = put("pool", lambda e: e.tensor_tensor(dst, ms[:, 0:m], NH[:, 0:m], ALU.pow), t1, pwfree["pw"],
                     pwfree["rcol"] if mark_rcol is not None else None)
            pwfree["ms"] = [t2]
            w = 128 // groups
            src = dst.rearrange("p (i g) -> p i g", g=groups).unsqueeze(3).to_broadcast([128, 4, groups, w])
            d4 = r4ap.rearrange("p (i g w) -> p i g w", i=4, g=groups)
            if groups == 1:
                src = dst.unsqueeze(2).to_broadcast([128, 4, 128])
                d4 = r4ap.rearrange("p (i w) -> p i w", i=4)
            t3 = put("dve", lambda e: e.tensor_copy(d4, src), t2, r4.free)
            if mark_rcol is None:
                pwfree["pw"] = [t3]
            return t2, t3

        pwfree = {"ms": [], "pw": [], "rcol": []}

        def spread(bk, r4, r4ap, tok):
            for i in range(4):
                t = pe_transpose(bk.ap[:, i * 128:(i + 1) * 128], r4ap[:, i * 128:(i + 1) * 128], ID,
                                 [tok, bk.free if i == 0 else None], i == 3)
            r4.free = [t]
            return t

        accx = {"tok": None}

        def x_norm_a():
            acc = S[5]
            r, t = inv_rms(bank[6], 1, D, accx["tok"], lambda i: acc.ap[:, i * 128:(i + 1) * 128], ONE, S[4], S[4].ap, 1,
                           mark_rcol=RCOL)
            acc.free = q.now()[:1]
            rbt["rcol"] = r
            rbt["r4"] = t

        def x_norm_b():
            t = spread(bank[6], S[4], S[4].ap, rbt["r4"])
            t2 = put("act", lambda e: e.activation(RB[:, :], bank[6].ap[:, :], ACT.Copy), t, rb.free)
            bank[6].free = [t2]
            rbt["rb"] = t2

        def barrier(snap):
            for e in ("act", "dve", "pool"):
                q.hold(e, [t for t in snap if t[0] != e])

        def x_post(ms, txs, gcol):
            ths = []
            for m, tx in zip(ms, txs):
                if gcol is None:
                    ths.append(put("act", lambda e: e.activation(XH[:, m, :], X[:, m, :], ACT.Copy), tx))
                else:
                    ths.append(put("act", lambda e: e.activation(XH[:, m, :], X[:, m, :], ACT.Copy, scale=gcol(m)), tx))
            for m, tx, th in zip(ms, txs, ths):
                if gcol is None:
                    tl = put("dve", lambda e: e.tensor_tensor(XL[:, m, :], X[:, m, :], F(XH[:, m, :]), ALU.subtract), th, tx)
                else:
                    tl = put("dve", lambda e: e.scalar_tensor_tensor(XL[:, m, :], X[:, m, :], gcol(m), F(XH[:, m, :]), ALU.mult, ALU.subtract), th, tx)
                xtok[m] = [th, tl]
            for m, tx in zip(ms, txs):
                square_x(m, tx)

        def square_x(m, tx):
            acc, sq = S[5], S[4]
            if m == 0:
                accx["tok"] = put("act", lambda e: e.activation(acc.ap, X[:, m, :], ACT.Square), tx, acc.free)
            else:
                ts = put("act", lambda e: e.activation(sq.ap, X[:, m, :], ACT.Square), tx, sq.free)
                accx["tok"] = put("pool", lambda e: e.tensor_tensor(acc.ap, acc.ap, sq.ap, ALU.add), ts, accx["tok"])
                sq.free = [accx["tok"]]

        def resid(ms, bs, toks, scale, gcol):
            txs = []
            for m, b, tok in zip(ms, bs, toks):
                tx = put("dve", lambda e: e.scalar_tensor_tensor(X[:, m, :], b.ap[:, :], scale, X[:, m, :], ALU.mult, ALU.add), tok)
                b.free = [tx]
                txs.append(tx)
            x_post(ms, txs, gcol)

        def gc(base):
            return lambda m: GA[:, base + m:base + m + 1]

        def plan_ffn(tag, wgu, wd):
            for c in range(NF // 2):
                if c == 0:
                    plan_two(f"{tag}g0", wgu, 0, f"{tag}u0", wgu, FF)
                    continue
                plan_cols(f"{tag}g{c}", wgu, c * 256)
                plan_cols(f"{tag}u{c}", wgu, FF + c * 256)
            for p in range(4):
                plan_cols(f"{tag}d{p}", wd, p * 256, nk=NF)

        def ffn(tag, snap, gnext):
            AH = AR[:, 0:NF * T].rearrange("p (f t) -> p f t", t=T)
            AL = AR[:, NF * T:2 * NF * T].rearrange("p (f t) -> p f t", t=T)
            atok = [None] * NF

            def evac(f, g, u, tg, tu):
                s, t_, w = S[f % 2], S[2 + f % 2], Buf(AF[:, (f % 2) * T:(f % 2) * T + T])
                w.free = wfree[f % 2]
                a1 = put("dve", lambda e: e.tensor_tensor(s.ap, g.ap[:, :], RB[:, :], ALU.mult), tg, rbt["rb"], s.free)
                g.free = [a1]
                a2 = put("act", lambda e: e.activation(t_.ap, s.ap, ACT.Tanh, scale=0.5), a1, t_.free)
                a3 = put("dve", lambda e: e.tensor_tensor(w.ap, u.ap[:, :], RB[:, :], ALU.mult), tu, w.free)
                u.free = [a3]
                return s, t_, w, a1, a2, a3

            def evac2(f, st):
                s, t_, w, a1, a2, a3 = st
                a4 = put("dve", lambda e: e.tensor_tensor(w.ap, s.ap, w.ap, ALU.mult), a1, a3)
                s.free = [a4]
                return a4

            def evac3(f, st, a4):
                s, t_, w, a1, a2, a3 = st
                a5 = put("dve", lambda e: e.scalar_tensor_tensor(w.ap, t_.ap, 1.0, w.ap, ALU.add, ALU.mult), a2, a4)
                t_.free = [a5]
                return put("act", lambda e: e.activation(AH[:, f, :], w.ap, ACT.Copy), a5), a5

            def evac4(f, st, a6, a5):
                w = st[2]
                a7 = put("dve", lambda e: e.tensor_tensor(AL[:, f, :], w.ap, F(AH[:, f, :]), ALU.subtract), a5, a6)
                wfree[f % 2] = [a7]
                atok[f] = [a6, a7]

            wfree = [[], []]

            def evac_pair(c, bs, tk):
                for j in range(2):
                    f = 2 * c + j
                    st = evac(f, bs[j], bs[2 + j], tk[j], tk[2 + j])
                    yield
                    a4 = evac2(f, st)
                    yield
                    r = evac3(f, st, a4)
                    yield
                    evac4(f, st, *r)
                    yield

            tk = [None] * 4
            drain(two_chunks(f"{tag}g0", f"{tag}u0", bank[0:4], xk, xtok, tk))
            x_norm_a()
            for c in range(1, NF // 2):
                bs = bank[4:8] if c % 2 else bank[0:4]
                t2 = []
                ga = tiles(f"{tag}g{c}", bs[0:2], xk, xtok, toks=t2)
                if c == 1:
                    for _ in range(8):
                        next(ga)
                    x_norm_b()
                    barrier(snap)
                    pend = stream(evac_pair(0, bank[0:4], tk), 0.3)
                weave(ga, pend)
                weave(tiles(f"{tag}u{c}", bs[2:4], xk, xtok, toks=t2), pend)
                finish(pend)
                pend = stream(evac_pair(c, bs, t2), 0.3)
            finish(pend)
            rb.free = q.now()

            def ak(k):
                return AH[:, k, :], AL[:, k, :]

            for p in range(4):
                o = (2 * p + 4) % 8
                bs = bank[o:o + 2]
                tk = []
                drain(tiles(f"{tag}d{p}", bs, ak, atok, toks=tk, nu=6))
                resid((2 * p, 2 * p + 1), bs, tk, 0.25, gnext)

        def split_scaled(src, h, l, scale, waits, free=()):
            t1 = put("act", lambda e: e.activation(h, src, ACT.Copy, scale=scale), waits, free)
            if isinstance(scale, float) and scale == 1.0:
                t2 = put("dve", lambda e: e.tensor_tensor(l, src, F(h), ALU.subtract), t1, waits, free)
            else:
                t2 = put("dve", lambda e: e.scalar_tensor_tensor(l, src, scale, F(h), ALU.mult, ALU.subtract), t1, waits, free)
            return [t1, t2]

        def split_bank(parts, waits, free=()):
            for src, h, l, sc in parts:
                t1 = put("act", lambda e, src=src, h=h, sc=sc: e.activation(h, src, ACT.Copy, scale=sc), waits, free)
            for src, h, l, sc in parts:
                t2 = put("dve", lambda e, src=src, h=h, l=l, sc=sc: e.scalar_tensor_tensor(l, src, sc, F(h), ALU.mult, ALU.subtract),
                         t1, waits, free)
            return [t1, t2]

        def evac_rb(b, tok, s, h, l, scale, free=()):
            t = put("dve", lambda e: e.tensor_tensor(s.ap, b.ap[:, :], RB[:, :], ALU.mult), tok, rbt["rb"], s.free)
            b.free = [t]
            r = split_scaled(s.ap, h, l, scale, [t], free)
            s.free = r
            return r

        def v_chunk(name, banks, lhs, ltok, nt, toks):
            w0, w1 = get((name, 0)), get((name, 1))
            for i in range(nt):
                b = banks[i // 2]
                for k in range(KT):
                    w = w0 if k < 4 else w1
                    lh, ll = lhs(k)
                    o = b.ap[:, (i % 2) * 256:(i % 2) * 256 + 256]
                    sl = slice(i * 128, i * 128 + 128)
                    t = mm3(o, lh[:, sl], ll[:, sl], w[0][:, k % 4, :], w[1][:, k % 4, :],
                            [w[2], ltok[k] if ltok else None, b.free if i % 2 == 0 and k == 0 else None],
                            k == 0, k == 7, mark=k == 7)
                    if k < KT - 1:
                        yield 1
                toks.append(t)
                if i == nt - 1:
                    done(w0, t)
                    done(w1, t)
                    pump()
                yield 1

        def evac_v(banks, toks, vh, vl, nt, scaled, free):
            r = []
            for n in range(nt // 2):
                b = banks[n]
                parts = [(b.ap[:, j * 256:j * 256 + 256], vh[:, 2 * n + j, :], vl[:, 2 * n + j, :],
                          RCOL[:, 2 * n + j:2 * n + j + 1] if scaled else 1.0) for j in range(2)]
                b.free = split_bank(parts, [toks[2 * n + 1], rbt["rcol"] if scaled else None], free)
                r += b.free
            return r

        def pT_views(off):
            h = AR[:, off:off + 1536].rearrange("p (j t) -> p j t", t=256)
            l = AR[:, off + 1536:off + 3072].rearrange("p (j t) -> p j t", t=256)
            return h, l

        def clear_pT(PH, PL):
            toks = []
            for j in (1, 5):
                for P_ in (PH, PL):
                    toks.append(put("dve", lambda e, P_=P_, j=j: e.memset(F(P_[:, j, 0:128]), 0.0)))
            return toks

        def softmax_row(sbk, n, tok, p, cq, mxc):
            mx, nb, ls = MX[:, mxc:mxc + 1], NB[:, mxc:mxc + 1], LS[:, mxc:mxc + 1]
            t1 = put("dve", lambda e: e.reduce_max(mx, sbk.ap[:, 0:n], AX), tok, smf[mxc])
            if cq is None:
                t2 = put("dve", lambda e: e.tensor_scalar(nb, mx, -1.0, None, ALU.mult), t1, smf[mxc])
            else:
                t2 = put("dve", lambda e: e.scalar_tensor_tensor(nb, mx, cq, cq, ALU.add, ALU.subtract, reverse1=True), t1, smf[mxc])
            t3 = put("act", lambda e: e.activation(p.ap[:, 0:n], sbk.ap[:, 0:n], ACT.Exp, bias=nb, accum_out=ls), t2, p.free, smf[mxc])
            sbk.free = [t3]
            smf[mxc] = [t3]
            return t3, ls

        smf = [[], [], [], []]

        def shape_load(n, col):
            s = (S[3], S[2])[n]
            return s, put("sp", lambda e: e.dma_start(s.ap[:, 0:128], consts[:, col:col + 128]), s.free, sem=f"sm{n}", by=16)

        def shape_matrix(dst, loaded, snap):
            s, d = loaded
            t = put("act", lambda e: e.activation(dst, s.ap[:, 0:128], ACT.Copy), d, snap)
            s.free = [t]
            return t

        def plan_mix(l):
            w, wo = a["w_mix_in"][l], a["w_mix_out"][l]
            t = f"m{l}"
            plan_two(t + "q0", w, 3 * CW, t + "k0", w, 4 * CW)
            plan_cols(t + "v0", w, 5 * CW)
            plan((t + "zf", 0), w[:, 6 * CW:6 * CW + 8].rearrange("(k p) c -> p k c", p=128), kind="pad")
            for h in range(2):
                if h == 1:
                    plan_cols(t + "q1", w, 3 * CW + 256)
                    plan_cols(t + "k1", w, 4 * CW + 256)
                plan_cols(t + f"zc{h}", w, CW + h * 256)
                plan_cols(t + f"zv{h}", w, 2 * CW + h * 256)
                plan_cols(t + f"zb{h}", w, h * 256)
                if h == 0:
                    plan_cols(t + "v1", w, 5 * CW + 256)
            plan_two(t + "o0", wo, 0, t + "o1", wo, 256)
            for p in (2, 3):
                plan_cols(t + f"o{p}", wo, p * 256)

        def mix(l, snap, gnext, mem_side):
            tg = f"m{l}"
            gco, gat = 80 + 4 * l, 88 + 4 * l
            YH = AR[:, 0:4096].rearrange("p (k t) -> p k t", t=T)
            YL = AR[:, 4096:8192].rearrange("p (k t) -> p k t", t=T)
            QK = AR[:, 8192:12288].rearrange("p (k t) -> p k t", t=T)
            QH, QL, KH, KL = QK[:, 0:2], QK[:, 2:4], QK[:, 4:6], QK[:, 6:8]
            VV = AR[:, 12288:16384].rearrange("p (s i c) -> p s i c", s=4, c=256)
            PH, PL = pT_views(16384)
            NCH, NCL = AR[0:8, 19456:19968], AR[0:8, 19968:20480]
            CB = [Buf(AF[:, i * T:i * T + T]) for i in range(2)]
            UB = [Buf(AF[:, 1024 + i * 514:1024 + i * 514 + 514]) for i in range(2)]
            RBC, RBA = AF[:, 2052:2564], AF[:, 2564:3076]
            CQ = AF[:, 3076:3108].rearrange("p (i h) -> p i h", h=8)
            tk = [None] * 4
            drain(two_chunks(tg + "q0", tg + "k0", bank[0:4], xk, xtok, tk))
            ld0 = shape_load(0, C_MQ)
            x_norm_a()
            vt = []
            g = v_chunk(tg + "v0", bank[4:6], xk, xtok, 4, vt)
            for _ in range(8):
                next(g)
            x_norm_b()
            drain(g)
            barrier(snap)
            MR = AR[:, 20480:20608]
            mrt = shape_matrix(MR, ld0, snap)
            ztok = clear_pT(PH, PL)
            for i in range(2):
                ztok.append(put("dve", lambda e, i=i: e.memset(UB[i].ap[:, 0:2], 0.0)))
            qkt = {}
            for i in range(4):
                h, lo = ((QH, QL), (KH, KL))[i // 2]
                qkt[i] = evac_rb(bank[i], tk[i], S[i % 2], h[:, i % 2, :], lo[:, i % 2, :], 0.125 if i < 2 else 1.0)
            vtok = [None, None]
            vtok[0] = evac_v(bank[4:6], vt, VV[:, 0], VV[:, 1], 4, True, ())
            w = get((tg + "zf", 0))
            for k in range(KT):
                t = mm3(bank[7].ap[:, :], w[0][:, k, :], w[1][:, k, :], XH[:, k, :], XL[:, k, :],
                        [w[2], xtok[k], bank[7].free if k == 0 else None], k == 0, k == 7, mark=k == 7)
            done(w, t)
            pump()
            zt = t

            def forget_gate():
                z, y, on = S[2], S[3], S[4]
                z8, y8, o8 = z.ap[0:8, :], y.ap[0:8, :], on.ap[0:8, :]
                t0 = put("dve", lambda e: e.memset(o8, 1.0), on.free)
                t = put("dve", lambda e: e.tensor_tensor(z8, bank[7].ap[0:8, :], RB[0:8, :], ALU.mult), zt, rbt["rb"], z.free)
                bank[7].free = [t]
                t = put("dve", lambda e: e.tensor_scalar(z8, z8, BF[0:8, l:l + 1], None, ALU.add), t)
                t1 = put("act", lambda e: e.activation(y8, z8, ACT.Abs), t, y.free)
                t1 = put("act", lambda e: e.activation(y8, y8, ACT.Exp, scale=-1.0), t1)
                t1 = put("act", lambda e: e.activation(y8, y8, ACT.Ln, bias=1.0), t1)
                t = put("dve", lambda e: e.scalar_tensor_tensor(z8, z8, 0.0, y8, ALU.min, ALU.subtract), t1, t)
                tc = put("dve", lambda e: e.tensor_tensor_scan(y8, o8, z8, 0.0, ALU.mult, ALU.add), t, t0, t1)
                st["nc"] = nct = split_scaled(y8, NCH, NCL, -1.0, [tc])
                yield from pause(8)
                for i in range(4):
                    tt = pe_transpose(bank[6].ap[:, i * 8:i * 8 + 8], y8[:, i * 128:(i + 1) * 128], ID[0:8, 0:8],
                                      [tc, bank[6].free if i == 0 else None], i == 3)
                tcq = put("dve", lambda e: e.tensor_copy(CQ[:, :, :], bank[6].ap[:, 0:32].rearrange("p (i h) -> p i h", h=8)), tt)
                bank[6].free = [tcq]
                z.free, y.free, on.free = [tc], [nct, tt], [tc]
                st["cq"] = tcq

            ytok = [None] * 8
            qkfree = []
            vfree = []
            st = {"acc": None, "pv": None}

            def att(quad):
                A_ = {}
                ev = {}

                def stage_a(n):
                    hq, i = divmod(n, 4)
                    tl, hh = divmod(hq, 2)
                    h = 4 * quad + hq
                    r = slice(64 * hh, 64 * hh + 64)
                    N = (i + 1) * 128
                    b = bank[4 + n % 2]
                    o = b.ap[:, 0:N]
                    qs = slice(i * 128, N)
                    mm3(o, QH[r, tl, qs], QL[r, tl, qs], KH[r, tl, 0:N], KL[r, tl, 0:N],
                        [qkt[tl], qkt[2 + tl], b.free], True, False)
                    e8 = IDR[0:8, h:h + 1].to_broadcast([8, 128])
                    mm(o, e8, NCH[:, 0:N], [st["nc"]], False, False, False)
                    mm(o, e8, NCL[:, 0:N], (), False, False, False)
                    t = mm(b.ap[:, N - 128:N], IDR[:, :], MR, [mrt], False, True, True)
                    qkfree.append(t)
                    p = S[2 + n % 2]
                    t3, ls = softmax_row(b, N, t, p, CQ[:, i, h:h + 1], n % 2)
                    rl = RL[:, n % 2:n % 2 + 1]
                    t4 = put("dve", lambda e: e.reciprocal(rl, ls), t3)
                    smf[n % 2] = [t3, t4]
                    t5 = put("dve", lambda e: e.tensor_scalar(p.ap[:, 0:N], p.ap[:, 0:N], rl, None, ALU.mult), t4, t3)
                    A_[n] = (p, t5, N)

                def stage_b(n):
                    hq, i = divmod(n, 4)
                    p, tp, N = A_.pop(n)
                    b = bank[6]
                    for j in range(i + 1):
                        t = pe_transpose(b.ap[:, j * 128:(j + 1) * 128], p.ap[:, j * 128:(j + 1) * 128], ID,
                                         [tp, b.free if j == 0 else None], j == i)
                    p.free = [t]
                    j0 = 0 if i < 2 else 2
                    src = b.ap[:, 0:N].rearrange("p (j t) -> p j t", t=128)
                    cs = slice((i % 2) * 128, (i % 2) * 128 + 128)
                    r = split_scaled(src, PH[:, j0:j0 + i + 1, cs], PL[:, j0:j0 + i + 1, cs], 1.0, [t], [st["pv"], ztok])
                    b.free = r
                    ev[n] = r

                def stage_c(hq):
                    tl, hh = divmod(hq, 2)
                    b = bank[7]
                    for a_ in range(2):
                        for j in range(2 * a_ + 2):
                            jj = (0 if a_ == 0 else 2) + j
                            t = mm3(b.ap[:, a_ * 256:a_ * 256 + 256], VV[:, 2 * quad, j, tl * 128:tl * 128 + 128],
                                    VV[:, 2 * quad + 1, j, tl * 128:tl * 128 + 128], PH[:, jj, :], PL[:, jj, :],
                                    [vtok[quad], ev[4 * hq + 2 * a_ + 1], ev[4 * hq + 2 * a_], b.free if j == 0 and a_ == 0 else None],
                                    j == 0, j == 2 * a_ + 1, mark=j == 2 * a_ + 1)
                    st["pv"] = t
                    r = slice(64 * hh, 64 * hh + 64)
                    kt = 4 + 2 * quad + tl
                    src = b.ap[r, :]
                    g_ = GA[r, gat + kt - 4:gat + kt - 3]
                    if kt == 4:
                        ts = put("act", lambda e: e.activation(RBA[r, :], src, ACT.Square), t)
                        st["acc%d" % hh] = ts
                    else:
                        sq = S[5]
                        ts = put("act", lambda e: e.activation(sq.ap[r, :], src, ACT.Square), t, sq.free)
                        ta = put("pool", lambda e: e.tensor_tensor(RBA[r, :], RBA[r, :], sq.ap[r, :], ALU.add), ts, st["acc%d" % hh])
                        sq.free = [ta]
                        st["acc%d" % hh] = ta
                    rr = split_scaled(src, YH[r, kt, :], YL[r, kt, :], g_, [t])
                    b.free = [ts, rr]
                    ytok[kt] = [ytok[kt], rr]

                for n in range(19):
                    if n >= 3 and (n - 3) % 4 == 3:
                        stage_c((n - 3) // 4)
                        yield
                    if 2 <= n <= 17:
                        stage_b(n - 2)
                        yield
                    if n < 16:
                        stage_a(n)
                        yield

            accc = {}

            ct = [None, None]

            def conv_c(tks):
                for j in range(2):
                    t = put("dve", lambda e: e.tensor_tensor(CB[j].ap, bank[j].ap[:, :], RB[:, :], ALU.mult), tks[j], rbt["rb"], CB[j].free)
                    bank[j].free = [t]
                    ct[j] = t
                    yield

            def conv_v(half, tks):
                for j in range(2):
                    m = 2 * half + j
                    wc = [GB[:, (l * 3 + kk) * 4 + m:(l * 3 + kk) * 4 + m + 1] for kk in range(3)]
                    s, u, c = S[j], UB[j], CB[j]
                    t = put("dve", lambda e: e.tensor_tensor(s.ap, bank[2 + j].ap[:, :], RB[:, :], ALU.mult), tks[j], s.free)
                    bank[2 + j].free = [t]
                    yield
                    t = put("dve", lambda e: e.tensor_tensor(u.ap[:, 2:514], s.ap, c.ap, ALU.mult), t, ct[j], u.free)
                    s.free = [t]
                    yield
                    t = put("dve", lambda e: e.tensor_scalar(c.ap, u.ap[:, 2:514], wc[2], None, ALU.mult), t, ztok)
                    yield
                    t = put("dve", lambda e: e.scalar_tensor_tensor(c.ap, u.ap[:, 1:513], wc[1], c.ap, ALU.mult, ALU.add), t)
                    yield
                    t = put("dve", lambda e: e.scalar_tensor_tensor(c.ap, u.ap[:, 0:512], wc[0], c.ap, ALU.mult, ALU.add), t)
                    u.free = [t]
                    ct[j] = t
                    yield

            def conv_b(half, tks):
                for j in range(2):
                    m = 2 * half + j
                    s, c = S[j], CB[j]
                    t = put("dve", lambda e: e.tensor_tensor(s.ap, bank[j].ap[:, :], RB[:, :], ALU.mult), tks[j], s.free)
                    bank[j].free = [t]
                    yield
                    t = put("dve", lambda e: e.tensor_tensor(s.ap, s.ap, c.ap, ALU.mult), t, ct[j])
                    c.free = [t]
                    yield
                    if m == 0:
                        ts = put("act", lambda e: e.activation(RBC, s.ap, ACT.Square), t)
                        accc["t"] = ts
                    else:
                        sq = S[4]
                        ts = put("act", lambda e: e.activation(sq.ap, s.ap, ACT.Square), t, sq.free)
                        ta = put("pool", lambda e: e.tensor_tensor(RBC, RBC, sq.ap, ALU.add), ts, accc["t"])
                        sq.free = [ta]
                        accc["t"] = ta
                    rr = split_scaled(s.ap, YH[:, m, :], YL[:, m, :], GA[:, gco + m:gco + m + 1], [t])
                    ytok[m] = rr
                    s.free = [rr, ts]
                    yield

            def qk_evac(nm, bb, tks):
                (h, lo), sc_, key = (((QH, QL), 0.125, 0), ((KH, KL), 1.0, 2))[nm == "k1"]
                for j in range(2):
                    qkt[key + j] = evac_rb(bank[bb + j], tks[j], S[j], h[:, j, :], lo[:, j, :], sc_, list(qkfree))
                    yield

            def chunk(nm, bb, side, prev, v=None):
                tks = []
                main = tiles(tg + nm, bank[bb:bb + 2], xk, xtok, toks=tks) if v is None else v_chunk(tg + nm, bank[bb:bb + 2], xk, xtok, 4, tks)
                if side is None:
                    weave(main, prev)
                else:
                    weave(main, side, prev)
                finish(prev)
                return tks

            none = stream(iter(()), 1)
            side = stream(chain(forget_gate(), att(0)), 0.4)
            next(side[0])
            t1 = chunk("zc0", 0, side, none)
            t2 = chunk("zv0", 2, side, stream(conv_c(t1), 0.3))
            t3 = chunk("zb0", 0, side, stream(conv_v(0, t2), 0.4))
            t4 = chunk("v1", 2, side, stream(conv_b(0, t3), 0.4), True)
            vtok[1] = evac_v(bank[2:4], t4, VV[:, 2], VV[:, 3], 4, True, ())
            t5 = chunk("q1", 0, side, none)
            finish(side)
            t6 = chunk("k1", 2, None, stream(qk_evac("q1", 0, t5), 0.3))
            side = stream(chain(qk_evac("k1", 2, t6), pause(3), att(1)), 0.4)
            next(side[0])
            t1 = chunk("zc1", 0, side, none)
            t2 = chunk("zv1", 2, side, stream(conv_c(t1), 0.3))
            t3 = chunk("zb1", 0, side, stream(conv_v(1, t2), 0.4))
            cb = stream(conv_b(1, t3), 0.4)
            rb.free = q.now()

            def norm_y(buf, acct, bk, r4):
                r, t = inv_rms(bk, 1, CW, acct, lambda i: buf[:, i * 128:(i + 1) * 128], ONE, r4, r4.ap, 1)
                pe = q.now()[:1]
                return t, pe

            def norm_y2(buf, bk, r4, t, pe):
                t = spread(bk, r4, r4.ap, t)
                t = put("act", lambda e: e.activation(buf, bk.ap[:, :], ACT.Copy), t, pe)
                bk.free = [t]
                return t

            def half(p, u, bs, k0):
                w = get((tg + f"o{p}", u))
                toks = []
                for k in range(4):
                    kk = k0 + k
                    for c in range(2):
                        b = bs[c]
                        t = mm3(b.ap[:, :], w[0][:, k, c * 128:(c + 1) * 128], w[1][:, k, c * 128:(c + 1) * 128],
                                YH[:, kk, :], YL[:, kk, :], [w[2], ytok[kk], b.free if k == 0 else None], k == 0, k == 3, mark=k == 3)
                        if k == 3:
                            toks.append(t)
                        if k == 3 and c == 1:
                            done(w, t)
                            pump()
                            res[(p, u)] = toks
                        yield 2

            res = {}
            side[1] = 0.4
            finish(cb)
            weave(half(0, 0, bank[0:2], 0), side)
            nc0 = norm_y(RBC, accc["t"], bank[6], S[4])
            weave(half(1, 0, bank[2:4], 0), side)
            finish(side)
            rc = norm_y2(RBC, bank[6], S[4], *nc0)
            na0 = norm_y(RBA, [st["acc0"], st["acc1"]], bank[7], S[5])
            drain(half(0, 1, bank[4:6], 4))
            ra = norm_y2(RBA, bank[7], S[5], *na0)

            def evac_o(m0):
                txs = []
                for m in (m0, m0 + 1):
                    bc, ba = bank[m % 4], bank[4 + m % 4]
                    p = m // 2
                    s0, s1 = S[2 * (m % 2)], S[2 * (m % 2) + 1]
                    t = put("dve", lambda e: e.tensor_tensor(s0.ap, bc.ap[:, :], RBC, ALU.mult), res[(p, 0)][m % 2], rc, s0.free)
                    bc.free = [t]
                    t2 = put("dve", lambda e: e.tensor_tensor(s1.ap, ba.ap[:, :], RBA, ALU.mult), res[(p, 1)][m % 2], ra, s1.free)
                    ba.free = [t2]
                    t = put("dve", lambda e: e.tensor_tensor(X[:, m, :], X[:, m, :], s0.ap, ALU.add), t)
                    s0.free = [t]
                    t = put("dve", lambda e: e.tensor_tensor(X[:, m, :], X[:, m, :], s1.ap, ALU.add), t, t2)
                    s1.free = [t]
                    txs.append(t)
                x_post((m0, m0 + 1), txs, gnext)

            evac_o(0)
            next(mem_side, None)
            drain(half(1, 1, bank[6:8], 4))
            evac_o(2)
            drain(mem_side)
            drain(half(2, 0, bank[0:2], 0))
            drain(half(2, 1, bank[4:6], 4))
            evac_o(4)
            drain(half(3, 0, bank[2:4], 0))
            drain(half(3, 1, bank[6:8], 4))
            evac_o(6)

        MH = AR[:, 8192:10240].rearrange("p (k t) -> p k t", t=256)
        ML = AR[:, 10240:12288].rearrange("p (k t) -> p k t", t=256)
        mtok = [None] * KT

        def mem_prep(l, gmem):
            us = [get((f"mem{l}", r)) for r in range(2)]
            s = S[0]
            nt = []
            for r in range(2):
                ap, tok, _ = us[r]
                row = ap.rearrange("p k c -> p (k c)")
                ts = []
                for hf in range(2):
                    ts.append(put("act", lambda e, r=r, hf=hf, row=row: e.activation(s.ap, row[:, hf * 512:hf * 512 + 512], ACT.Square,
                                  accum_out=MSS[:, 2 * r + hf:2 * r + hf + 1]), tok, s.free, ts))
                s.free = [ts]
                t = put("dve", lambda e, r=r: e.tensor_tensor(MS[:, r:r + 1], MSS[:, 2 * r:2 * r + 1], MSS[:, 2 * r + 1:2 * r + 2], ALU.add), ts, pwfree["ms"])
                t = put("dve", lambda e, r=r: e.tensor_scalar(MS[:, r:r + 1], MS[:, r:r + 1], 1.0 / D, EPS, ALU.mult, ALU.add), t)
                t = put("pool", lambda e, r=r: e.tensor_tensor(PW[:, r:r + 1], MS[:, r:r + 1], NH[:, 0:1], ALU.pow), t, pwfree["pw"])
                t = put("dve", lambda e, r=r, row=row: e.tensor_scalar(row, row, PW[:, r:r + 1], None, ALU.mult), t, ts)
                nt.append(t)
            pwfree["ms"] = [t]
            pwfree["pw"] = [t]
            yield
            b = bank[6]
            for k2 in range(4):
                bb = bank[6 + k2 % 2]
                for j in range(2):
                    for r in range(2):
                        row = us[r][0].rearrange("p k c -> p (k c)")
                        k = 2 * k2 + j
                        t = pe_transpose(bb.ap[:, j * 256 + r * 128:j * 256 + r * 128 + 128], row[:, k * 128:(k + 1) * 128], ID,
                                         [nt, bb.free if j == 0 and r == 0 else None], j == 1 and r == 1)
                bb.free = split_bank([(bb.ap[:, j * 256:j * 256 + 256], MH[:, 2 * k2 + j, :], ML[:, 2 * k2 + j, :],
                                       GA[:, gmem + 2 * k2 + j:gmem + 2 * k2 + j + 1]) for j in range(2)], [t])
                mtok[2 * k2] = mtok[2 * k2 + 1] = bb.free
                if k2 == 3:
                    for r in range(2):
                        raw_done(us[r], [t, nt[r]])
                    pump()
                yield

        def plan_x(l):
            wq, wkv, wo = a["w_xq"][l], a["w_xkv"][l], a["w_xo"][l]
            for h in range(4):
                plan_cols(f"x{l}k{h}", wkv, h * 256)
                plan_cols(f"x{l}v{h}", wkv, D + h * 256)
                plan_cols(f"x{l}q{h}", wq, h * 256)
            plan_two(f"x{l}o0", wo, 0, f"x{l}o1", wo, 256)
            for p in (2, 3):
                plan_cols(f"x{l}o{p}", wo, p * 256)

        def xattn(l, snap, gnext):
            tg = f"x{l}"
            OH = AR[:, 0:4096].rearrange("p (k t) -> p k t", t=T)
            OL = AR[:, 4096:8192].rearrange("p (k t) -> p k t", t=T)
            KV = AR[:, 12288:16384].rearrange("p (s i c) -> p s i c", s=8, c=256)
            QX = AR[:, 16384:20480].rearrange("p (s t) -> p s t", t=T)
            PT = AR[:, 20480:22528].rearrange("p (s t) -> p s t", t=T)
            PH, PL = PT[:, 0:2, :], PT[:, 2:4, :]
            otok = [None] * 8
            st = {"pv": None, "sc": [None, None], "vr": [None, None]}
            hd = {}

            def att(h):
                par = h % 2
                KH, KL, VH, VL = (KV[:, 4 * par + j] for j in range(4))
                QH, QL = QX[:, 4 * par:4 * par + 2, :], QX[:, 4 * par + 2:4 * par + 4, :]
                A_, ev = {}, {}

                def stage_a(i):
                    b = bank[4 + i % 2]
                    qs = slice(i * 128, i * 128 + 128)
                    for d in range(2):
                        t = mm3(b.ap[:, 0:256], QH[:, d, qs], QL[:, d, qs], KH[:, d, :], KL[:, d, :],
                                [hd[h]["q"], hd[h]["k"], b.free], d == 0, d == 1, mark=d == 1)
                    st["sc"][par] = t
                    p = S[2 + i % 2]
                    t3, ls = softmax_row(b, 256, t, p, None, i % 2)
                    rl = RL[:, i % 2:i % 2 + 1]
                    t4 = put("dve", lambda e: e.reciprocal(rl, ls), t3)
                    smf[i % 2] = [t3, t4]
                    t5 = put("dve", lambda e: e.tensor_scalar(p.ap[:, 0:256], p.ap[:, 0:256], rl, None, ALU.mult), t4, t3)
                    A_[i] = (p, t5)

                def stage_b(i):
                    p, tp = A_[i]
                    b = bank[6]
                    for j in range(2):
                        t = pe_transpose(b.ap[:, j * 128:(j + 1) * 128], p.ap[:, j * 128:(j + 1) * 128], ID,
                                         [tp, b.free if j == 0 else None], j == 1)
                    p.free = [t]
                    src = b.ap[:, 0:256].rearrange("p (j t) -> p j t", t=128)
                    qs = slice(i * 128, i * 128 + 128)
                    ev[i] = split_scaled(src, PH[:, :, qs], PL[:, :, qs], 1.0, [t], [st["pv"]])
                    b.free = ev[i]

                def stage_c(d):
                    b = bank[7]
                    for j in range(2):
                        t = mm3(b.ap[:, :], VH[:, j, d * 128:(d + 1) * 128], VL[:, j, d * 128:(d + 1) * 128], PH[:, j, :], PL[:, j, :],
                                [hd[h]["v"], list(ev.values()), b.free if j == 0 else None], j == 0, j == 1, mark=j == 1)
                    if d == 1:
                        st["pv"] = t
                        st["vr"][par] = t
                    rr = split_scaled(b.ap[:, :], OH[:, 2 * h + d, :], OL[:, 2 * h + d, :], 1.0, [t])
                    b.free = rr
                    otok[2 * h + d] = rr

                for n in range(6):
                    if n >= 2:
                        stage_b(n - 2)
                        yield
                    if n < 4:
                        stage_a(n)
                        yield
                stage_c(0)
                yield
                stage_c(1)
                yield

            side = stream(iter(()), 1)
            pend = stream(iter(()), 1)
            mk = lambda k: (MH[:, k, :], ML[:, k, :])

            def evac_k(h, tk, KH, KL, par):
                hd[h] = {"k": []}
                for j in range(2):
                    r = split_scaled(bank[j].ap[:, 0:256], KH[:, j, :], KL[:, j, :], 1.0, [tk[j]], [st["sc"][par]])
                    bank[j].free = r
                    hd[h]["k"] += r
                    yield

            def evac_q(h, tk, bs, QH, QL, par):
                hd[h]["q"] = []
                for j in range(2):
                    hd[h]["q"] += evac_rb(bs[j], tk[j], S[j], QH[:, j, :], QL[:, j, :], 1.0 / 16.0, [st["sc"][par]])
                    yield

            for h in range(4):
                par = h % 2
                KH, KL, VH, VL = (KV[:, 4 * par + j] for j in range(4))
                QH, QL = QX[:, 4 * par:4 * par + 2, :], QX[:, 4 * par + 2:4 * par + 4, :]
                vb = bank[4:5] if h == 0 else bank[2:3]
                qb = bank[2:4] if h == 0 else bank[0:2]
                tk = []
                weave(tiles(tg + f"k{h}", bank[0:2], mk, mtok, toks=tk, n=256), side, pend)
                finish(pend)
                if h == 0:
                    barrier(snap)
                kp = stream(evac_k(h, tk, KH, KL, par), 0.3)
                vt = []
                weave(v_chunk(tg + f"v{h}", vb, mk, mtok, 2, vt), side, kp)
                finish(kp)
                if h == 0:
                    x_norm_a()
                tk = []
                hd[h]["v"] = evac_v(vb, vt, VH, VL, 2, False, [st["vr"][par]])
                gq = tiles(tg + f"q{h}", qb, xk, xtok, toks=tk)
                if h == 0:
                    for _ in range(8):
                        next(gq)
                    x_norm_b()
                weave(gq, side)
                finish(side)
                pend = stream(evac_q(h, tk, qb, QH, QL, par), 0.3)
                next(pend[0])
                next(pend[0])
                side = stream(att(h), 0.18)
            finish(pend)
            rb.free = q.now()

            def ok(k):
                return OH[:, k, :], OL[:, k, :]

            side[1] = 0.3
            out_proj(tg, ok, otok, gnext, side)

        def out_proj(tg, ok, otok, gnext, side, fin=False):
            tk = [None] * 4
            g = two_chunks(tg + "o0", tg + "o1", bank[0:4], ok, otok, tk)

            def early():
                for y in g:
                    if y == 0:
                        return
                    yield y

            weave(early(), side)
            finish(side)
            drain(g)
            for m in (0, 2):
                resid((m, m + 1), bank[m:m + 2], tk[m:m + 2], 1.0, gnext) if not fin else fin_tile(m, bank[m:m + 2], tk[m:m + 2])
            for p in (2, 3):
                bs = bank[2 * p:2 * p + 2]
                tk = []
                main = tiles(tg + f"o{p}", bs, ok, otok, toks=tk)
                if fin:
                    weave(main, stream(chain(store(0), store(1)) if p == 2 else store(2), 0.4))
                else:
                    drain(main)
                m = 2 * p
                resid((m, m + 1), bs, tk, 1.0, gnext) if not fin else fin_tile(m, bs, tk)
            if fin:
                drain(store(3))

        def fin_tile(m0, bs, toks):
            for m, b, tok in zip((m0, m0 + 1), bs, toks):
                tx = put("dve", lambda e: e.scalar_tensor_tensor(X[:, m, :], b.ap[:, :], 1.0, X[:, m, :], ALU.mult, ALU.add), tok)
                b.free = [tx]
                xlast[m] = tx

        xlast = [None] * KT

        outs = []

        def store(p):
            for hf in range(2):
                b = bank[hf + 2 * (p % 2)]
                for j in range(2):
                    for c in range(2):
                        i = 2 * hf + j
                        t = pe_transpose(b.ap[:, j * 256 + c * 128:j * 256 + c * 128 + 128], X[:, 2 * p + c, i * 128:(i + 1) * 128], ID,
                                         [xlast[2 * p + c], b.free if j == 0 and c == 0 else None], j == 1 and c == 1)
                s = S[(2 * p + hf) % 4]
                yield
                if hf:
                    t = put("act", lambda e: e.activation(s.ap, b.ap[:, :], ACT.Copy), t, s.free)
                else:
                    t = put("dve", lambda e: e.tensor_copy(s.ap, b.ap[:, :]), t, s.free)
                b.free = [t]
                dst = out[0, hf * 256:hf * 256 + 256, p * 256:p * 256 + 256].rearrange("(j q) c -> q j c", j=2)
                tw = put("sp", lambda e: e.dma_start(dst, s.ap.rearrange("q (j c) -> q j c", j=2)), t, sem=f"out{(2 * p + hf) % 4}", by=16)
                s.free = [tw]
                outs.append(tw)
                yield

        def plan_diff():
            w, wo = a["a_w_in_2"][0], a["a_w_out_2"][0]
            plan_two("dq0", w, 0, "dk0", w, D)
            plan_cols("dv0", w, 2 * D)
            plan_cols("dv1", w, 2 * D + 256)
            for t in range(1, 4):
                if t > 1:
                    plan_cols(f"dv{t}", w, 2 * D + t * 256)
                plan_cols(f"dg{t - 1}", w, 3 * D + (t - 1) * 256)
                plan_cols(f"dq{t}", w, t * 256)
                plan_cols(f"dk{t}", w, D + t * 256)
            plan_cols("dg3", w, 3 * D + 3 * 256)
            plan_two("do0", wo, 0, "do1", wo, 256)
            for p in (2, 3):
                plan_cols(f"do{p}", wo, p * 256)

        def gate_evac(bs, tk, G, gfree, tmps, gtok, n):
            ts, t1, r = [None, None], [None, None], []
            for j in range(2):
                ts[j] = put("dve", lambda e: e.tensor_tensor(G[j], bs[j].ap[:, :], RB[:, :], ALU.mult), tk[j], rbt["rb"], gfree)
                bs[j].free = [ts[j]]
            yield
            for j in range(2):
                t1[j] = put("act", lambda e: e.activation(tmps[j].ap, G[j], ACT.Tanh, scale=0.5), ts[j], tmps[j].free)
            yield
            for j in range(2):
                t2 = put("dve", lambda e: e.scalar_tensor_tensor(G[j], tmps[j].ap, 1.0, G[j], ALU.add, ALU.mult), t1[j], ts[j])
                tmps[j].free = [t2]
                r.append(t2)
            gtok[n] = r
            yield

        def diff(snap, gnext):
            OH = AR[:, 0:4096].rearrange("p (k t) -> p k t", t=T)
            OL = AR[:, 4096:8192].rearrange("p (k t) -> p k t", t=T)
            QK = AR[:, 8192:12288].rearrange("p (k t) -> p k t", t=T)
            QH, QL, KH, KL = QK[:, 0:2], QK[:, 2:4], QK[:, 4:6], QK[:, 6:8]
            VV = AR[:, 12288:16384].rearrange("p (s i c) -> p s i c", s=4, c=256)
            PH, PL = pT_views(16384)
            G = [AF[:, i * T:i * T + T] for i in range(2)]
            COS, SIN = AF[:, 2048:2560], AF[:, 2560:3072]
            tk = [None] * 4
            drain(two_chunks("dq0", "dk0", bank[0:4], xk, xtok, tk))
            ld0, ld1 = shape_load(0, C_MQ), shape_load(1, C_ROT)
            x_norm_a()
            vt = []
            g = v_chunk("dv0", bank[4:6], xk, xtok, 4, vt)
            next(g)
            x_norm2_a()
            drain(g)
            x_norm2_b()
            barrier(snap)
            ct = [put("sp", lambda e: e.dma_start(AF[:, 2048:3072], consts[:, C_COS:C_COS + 2 * T]), snap, sem="c1", by=16)]
            MR = AR[:, 19456:19584]
            mrt = shape_matrix(MR, ld0, snap)
            ROT = AR[:, 19584:19712]
            rott = shape_matrix(ROT, ld1, snap)
            ztok = clear_pT(PH, PL)
            qkt = [None] * 4
            qkfree = []
            vtok = [None] * 4
            gtok = [None] * 4
            vtok[0] = evac_v(bank[4:6], vt, VV[:, 0], VV[:, 1], 4, True, ())
            st = {"pv": None, "prev": []}
            gfree = []
            otok = [None] * 8

            P1 = [S[3], Buf(AF[:, 1024:1536])]
            CT = [S[2], Buf(AF[:, 1536:2048])]
            CM = [MS[:, 0:8], SM[:, 61:69]]
            CP = [PW[:, 0:8], SM[:, 72:80]]

            def qk_chain(which, bs, tk, gain):
                H_, L_ = ((QH, QL), (KH, KL))[which]
                tps = CT
                tq, t, t1, t3, t4, t5, t6, t7, t8 = ([None, None] for _ in range(9))
                for j in range(2):
                    s = S[j]
                    tq[j] = put("dve", lambda e: e.tensor_tensor(s.ap, bs[j].ap[:, :], RB[:, :], ALU.mult), tk[j], rbt["rb"], s.free)
                    bs[j].free = [tq[j]]
                yield
                for j in range(2):
                    s, tp = S[j], tps[j]
                    t[j] = put("act", lambda e: e.activation(tp.ap, s.ap, ACT.Square), tq[j], tp.free)
                yield
                for j in range(2):
                    tp = tps[j]
                    for i in range(4):
                        t1[j] = mm(bs[j].ap[:, i * 2:i * 2 + 2], tp.ap[:, i * 128:(i + 1) * 128], BLK, [t[j], bs[j].free if i == 0 else None], mark=i == 3)
                    yield
                for j in range(2):
                    t2 = put("dve", lambda e: e.tensor_scalar(CM[j], bs[j].ap[:, 0:8], 1.0 / 64, EPS, ALU.mult, ALU.add), t1[j])
                    t3[j] = put("pool", lambda e: e.tensor_tensor(CP[j], CM[j], NH[:, 0:8], ALU.pow), t2)
                    bs[j].free = [t2]
                yield
                for j in range(2):
                    tp = tps[j]
                    src = CP[j].unsqueeze(2).to_broadcast([128, 8, 64])
                    t4[j] = put("dve", lambda e: e.tensor_copy(tp.ap.rearrange("p (g w) -> p g w", w=64), src), t3[j], t1[j])
                yield
                for j in range(2):
                    s, tp = S[j], tps[j]
                    for i in range(4):
                        t5[j] = pe_transpose(bs[j].ap[:, i * 128:(i + 1) * 128], tp.ap[:, i * 128:(i + 1) * 128], ID,
                                             [t4[j], bs[j].free if i == 0 else None], i == 3)
                    t6[j] = put("dve", lambda e: e.scalar_tensor_tensor(s.ap, s.ap, gain, bs[j].ap[:, :], ALU.mult, ALU.mult), t5[j], tq[j])
                    yield
                for j in range(2):
                    s, tp = S[j], tps[j]
                    t7[j] = mm(bs[j].ap[:, :], F(ROT), s.ap, [t6[j], rott])
                    t8[j] = put("pool", lambda e: e.tensor_tensor(tp.ap, s.ap, COS, ALU.mult), t6[j], t5[j], ct)
                    yield
                for j in range(2):
                    s, tp = S[j], tps[j]
                    t9 = put("dve", lambda e: e.tensor_tensor(s.ap, bs[j].ap[:, :], SIN, ALU.mult), t7[j], t8[j])
                    bs[j].free = [t9]
                    t10 = put("dve", lambda e: e.tensor_tensor(s.ap, s.ap, tp.ap, ALU.add), t9)
                    tp.free = [t10]
                    r = split_scaled(s.ap, H_[:, j, :], L_[:, j, :], 1.0, [t10], st["prev"])
                    s.free = r
                    qkt[2 * which + j] = r
                    yield

            def att(pair):
                A_, ev = {}, {}
                mine = []

                def stage_a(n, c):
                    hq, i = divmod(n, 4)
                    N = (i + 1) * 128
                    qs = slice(i * 128, N)
                    r = slice(64 * c, 64 * c + 64)
                    b = bank[4 + c]
                    mm3(b.ap[:, 0:N], QH[r, hq, qs], QL[r, hq, qs], KH[r, hq, 0:N], KL[r, hq, 0:N],
                        [qkt[hq], qkt[2 + hq], b.free], True, False)
                    t = mm(b.ap[:, N - 128:N], IDR[:, :], MR, [mrt], False, True, True)
                    mine.append(t)
                    t3 = softmax_row(b, N, t, (P1[n % 2], S[4])[c], None, c)[0]
                    A_.setdefault(n, []).append(t3)

                def stage_a2(n):
                    N = (n % 4 + 1) * 128
                    t3s = A_[n]
                    t4 = put("dve", lambda e: e.reciprocal(RL[:, 0:2], LS[:, 0:2]), t3s)
                    smf[0], smf[1] = [t3s[0], t4], [t3s[1], t4]
                    t5 = put("dve", lambda e: e.tensor_tensor(NL, RL[:, 1:2], LAM, ALU.mult), t4, lamtok)
                    p1, p2 = P1[n % 2], S[4]
                    t6 = put("dve", lambda e: e.tensor_scalar(p2.ap[:, 0:N], p2.ap[:, 0:N], NL, None, ALU.mult), t5, t3s)
                    t7 = put("dve", lambda e: e.scalar_tensor_tensor(p1.ap[:, 0:N], p1.ap[:, 0:N], RL[:, 0:1], p2.ap[:, 0:N], ALU.mult, ALU.add), t6)
                    p2.free = [t7]
                    A_[n] = (p1, t7, N)

                def stage_b(n):
                    hq, i = divmod(n, 4)
                    p, tp, N = A_.pop(n)
                    b = bank[6]
                    for j in range(i + 1):
                        t = pe_transpose(b.ap[:, j * 128:(j + 1) * 128], p.ap[:, j * 128:(j + 1) * 128], ID,
                                         [tp, b.free if j == 0 else None], j == i)
                    p.free = [t]
                    j0 = 0 if i < 2 else 2
                    src = b.ap[:, 0:N].rearrange("p (j t) -> p j t", t=128)
                    cs = slice((i % 2) * 128, (i % 2) * 128 + 128)
                    ev[n] = split_scaled(src, PH[:, j0:j0 + i + 1, cs], PL[:, j0:j0 + i + 1, cs], 1.0, [t], [st["pv"], ztok])
                    b.free = ev[n]

                def stage_c(hq):
                    par = pair % 2
                    b = bank[7]
                    for a_ in range(2):
                        for j in range(2 * a_ + 2):
                            jj = (0 if a_ == 0 else 2) + j
                            t = mm3(b.ap[:, a_ * 256:a_ * 256 + 256], VV[:, 2 * par, j, hq * 128:hq * 128 + 128],
                                    VV[:, 2 * par + 1, j, hq * 128:hq * 128 + 128], PH[:, jj, :], PL[:, jj, :],
                                    [vtok[pair], ev[4 * hq + 2 * a_ + 1], ev[4 * hq + 2 * a_], b.free if j == 0 and a_ == 0 else None],
                                    j == 0, j == 2 * a_ + 1, mark=j == 2 * a_ + 1)
                    st["pv"] = t
                    return t

                def o_chain(hq, t):
                    h = 2 * pair + hq
                    b, s, x = bank[7], S[5], bank[6]
                    ts = put("act", lambda e: e.activation(s.ap, b.ap[:, :], ACT.Square), t, s.free)
                    yield
                    for i in range(4):
                        t1 = mm(x.ap[:, i:i + 1], s.ap[:, i * 128:(i + 1) * 128], ONE, [ts, x.free if i == 0 else None], mark=i == 3)
                    t2 = put("dve", lambda e: e.tensor_scalar(MSS, x.ap[:, 0:4], 1.0 / 128, EPS, ALU.mult, ALU.add), t1)
                    x.free = [t2]
                    t3 = put("pool", lambda e: e.tensor_tensor(LT, MSS, NH[:, 0:4], ALU.pow), t2)
                    t4 = put("pool", lambda e: e.tensor_copy(s.ap.rearrange("p (i w) -> p i w", i=4), LT.unsqueeze(2).to_broadcast([128, 4, 128])), t3, t1)
                    yield
                    t5 = spread(x, Buf(None), s.ap, t4)
                    t6 = put("act", lambda e: e.activation(s.ap, x.ap[:, :], ACT.Copy), t5)
                    x.free = [t6]
                    t7 = put("dve", lambda e: e.scalar_tensor_tensor(s.ap, b.ap[:, :], SG, s.ap, ALU.mult, ALU.mult), t6)
                    b.free = [t7]
                    g_ = G[hq]
                    assert gtok[pair] is not None
                    t8 = put("pool", lambda e: e.tensor_tensor(s.ap, s.ap, g_, ALU.mult), t7, gtok[pair][hq])
                    gfree.append(t8)
                    yield
                    t9 = put("act", lambda e: e.activation(OH[:, h, :], s.ap, ACT.Copy), t8)
                    r = [t9, put("pool", lambda e: e.tensor_tensor(OL[:, h, :], s.ap, F(OH[:, h, :]), ALU.subtract), t9)]
                    s.free = r
                    otok[h] = r
                    yield

                oc = iter(())
                for n in range(11):
                    if n >= 3 and (n - 3) % 4 == 3:
                        drain(oc)
                        oc = o_chain((n - 3) // 4, stage_c((n - 3) // 4))
                        next(oc)
                        yield
                    if 2 <= n <= 9:
                        stage_b(n - 2)
                    if 1 <= n <= 8:
                        stage_a2(n - 1)
                    yield
                    next(oc, None)
                    for c in range(2 if n < 8 else 0):
                        stage_a(n, c)
                        yield
                for _ in oc:
                    yield
                st["prev"] = mine

            def qc(bs, toks):
                assert len(toks) >= 2
                yield from qk_chain(0, bs, toks, QG)

            side = stream(chain(qk_chain(0, bank[0:2], tk[0:2], QG), qk_chain(1, bank[2:4], tk[2:4], GB[:, 26:27])), 0.75)
            vt = []
            weave(v_chunk("dv1", bank[6:8], xk, xtok, 4, vt), side)
            finish(side)
            vtok[1] = evac_v(bank[6:8], vt, VV[:, 2], VV[:, 3], 4, True, [])
            for t in range(1, 4):
                if t > 1:
                    vt = []
                    weave(v_chunk(f"dv{t}", bank[0:2], xk, xtok, 4, vt), side)
                    finish(side)
                    vs = 2 * (t % 2)
                    vtok[t] = evac_v(bank[0:2], vt, VV[:, vs], VV[:, vs + 1], 4, True, [st["pv"]])
                g2, tq, tk2 = [], [], []
                side = stream(chain(att(t - 1), qc(bank[0:2], tq)), 0.48)
                weave(tiles(f"dg{t - 1}", bank[2:4], xk, xtok, toks=g2), side)
                gg = stream(gate_evac(bank[2:4], g2, G, list(gfree), (S[5], S[2]), gtok, t - 1), 0.5)
                weave(tiles(f"dq{t}", bank[0:2], xk, xtok, toks=tq), gg, side)
                weave(tiles(f"dk{t}", bank[2:4], xk, xtok, toks=tk2), side)
                finish(side)
                side = stream(qk_chain(1, bank[2:4], tk2, GB[:, 26:27]), 0.4)
            g2 = []
            side = stream(chain(side[0], att(3)), 0.7)
            weave(tiles("dg3", bank[0:2], xk, xtok, toks=g2), side)
            drain(gate_evac(bank[0:2], g2, G, list(gfree), (S[5], S[2]), gtok, 3))
            side[1] = 0.45
            rb.free = q.now()

            def ok(k):
                return OH[:, k, :], OL[:, k, :]

            out_proj("d", ok, otok, gnext, side)

        def x_norm2_a():
            x_norm_b()
            tr = rbt["rb"]
            for m in range(KT):
                g_ = GA[:, 96 + m:97 + m]
                tx = put("dve", lambda e, m=m, g_=g_: e.scalar_tensor_tensor(X[:, m, :], X[:, m, :], g_, RB[:, :], ALU.mult, ALU.mult), tr, xtok[m])
                square_x(m, tx)

        def x_norm2_b():
            r1 = RL
            t = put("dve", lambda e: e.tensor_copy(LT[:, 0:4], RCOL), rbt["rcol"])
            acc = S[5]
            pwfree["rcol"] = [t]
            for i in range(4):
                tt = mm(bank[6].ap[:, i:i + 1], acc.ap[:, i * 128:(i + 1) * 128], ONE, [accx["tok"], bank[6].free if i == 0 else None], mark=i == 3)
            acc.free = [tt]
            t1 = put("dve", lambda e: e.tensor_scalar(MS[:, 0:4], bank[6].ap[:, 0:4], 1.0 / D, EPS, ALU.mult, ALU.add), tt, pwfree["ms"])
            bank[6].free = [t1]
            t2 = put("pool", lambda e: e.tensor_tensor(PW[:, 0:4], MS[:, 0:4], NH[:, 0:4], ALU.pow), t1, pwfree["pw"])
            pwfree["ms"] = [t2]
            t3 = put("dve", lambda e: e.tensor_tensor(RCOL, PW[:, 0:4], LT[:, 0:4], ALU.mult), t2, t, q.now()[2])
            pwfree["pw"] = [t3]
            rbt["rcol"] = t3
            s = S[4]
            t4 = put("dve", lambda e: e.tensor_copy(s.ap.rearrange("p (i w) -> p i w", i=4), RCOL.unsqueeze(2).to_broadcast([128, 4, 128])), t3, s.free)
            rb.free = q.now()
            t5 = spread(bank[6], s, s.ap, t4)
            t6 = put("act", lambda e: e.activation(RB[:, :], bank[6].ap[:, :], ACT.Copy), t5, rb.free)
            bank[6].free = [t6]
            rbt["rb"] = t6

        def plan_sb():
            wkv, w, wo = a["w_kv_2"], a["b_w_in_2"][0], a["b_w_out_2"][0]
            gk, gb = 112, 120
            plan_two("sq0", w, 0, "sk0", wkv, 0, gb, gk)
            plan_cols("sv0", wkv, D, gain=gk)
            plan_cols("sg0", w, D, gain=gb)
            for t in range(1, 4):
                plan_cols(f"sv{t}", wkv, D + t * 256, gain=gk)
                if t < 3:
                    plan_cols(f"sg{t}", w, D + t * 256, gain=gb)
                plan_cols(f"sq{t}", w, t * 256, gain=gb)
                plan_cols(f"sk{t}", wkv, t * 256, gain=gk)
            plan_cols("sg3", w, D + 3 * 256, gain=gb)
            plan_two("so0", wo, 0, "so1", wo, 256)
            for p in (2, 3):
                plan_cols(f"so{p}", wo, p * 256)

        def stick(snap):
            OH = AR[:, 0:4096].rearrange("p (k t) -> p k t", t=T)
            OL = AR[:, 4096:8192].rearrange("p (k t) -> p k t", t=T)
            QK = AR[:, 8192:12288].rearrange("p (k t) -> p k t", t=T)
            QH, QL, KH, KL = QK[:, 0:2], QK[:, 2:4], QK[:, 4:6], QK[:, 6:8]
            VV = AR[:, 12288:16384].rearrange("p (s i c) -> p s i c", s=4, c=256)
            LO = [[0, 512, 896, 1152], [0, 512, 896, 1280]]
            LH, LL = AR[:, 16384:17792], AR[:, 17792:19200]
            EH = [AR[:, 19200 + i * T:19200 + (i + 1) * T] for i in range(2)]
            EL = [AR[:, 20224 + i * T:20224 + (i + 1) * T] for i in range(2)]
            TRI = AR[:, 21248:21376]
            NEG = AR[:, 21376:21504]
            G = [AF[:, i * T:i * T + T] for i in range(4)]
            TMP = AF[:, 2048:2304]
            tk = [None] * 4
            drain(two_chunks("sq0", "sk0", bank[0:4], xk, xtok, tk))
            ld0, ld1 = shape_load(0, C_MK), shape_load(1, C_TRI)
            x_norm_a()
            vt = []
            g = v_chunk("sv0", bank[4:6], xk, xtok, 4, vt)
            next(g)
            x_norm_b()
            drain(g)
            barrier(snap)
            MR = AR[:, 21504:21632]
            ct = [shape_matrix(MR, ld0, snap), shape_matrix(TRI, ld1, snap)]
            c2 = put("dve", lambda e: e.memset(TMP[:, 0:128], -1.0))
            ct.append(put("act", lambda e: e.activation(NEG, TMP[:, 0:128], ACT.Copy), c2))
            qkt = [evac_rb(bank[i], tk[i], S[i % 2], (QH, KH)[i // 2][:, i % 2, :], (QL, KL)[i // 2][:, i % 2, :],
                           0.125 if i < 2 else 1.0) for i in range(4)]
            vtok, gtok = [None] * 4, [None] * 4
            vtok[0] = evac_v(bank[4:6], vt, VV[:, 0], VV[:, 1], 4, True, ())
            otok = [None] * 8
            st = {"prev": [], "pvs": [None, None], "lr": [None] * 5, "er": [[], []]}
            gfree = [[], []]

            def att(quad):
                mine = []
                par = quad % 2
                gfree[par] = []
                Z, E_ = {}, {}
                lt = {}

                def stage_a(n):
                    hq, jr = divmod(n, 4)
                    j = 3 - jr
                    tl, hh = divmod(hq, 2)
                    r = slice(64 * hh, 64 * hh + 64)
                    N = T - 128 * j
                    b = bank[4 + n % 3]
                    o = b.ap[:, 0:N]
                    ks = slice(j * 128, j * 128 + 128)
                    qs = slice(j * 128, T)
                    t = mm3(o, KH[r, tl, ks], KL[r, tl, ks], QH[r, tl, qs], QL[r, tl, qs], [qkt[tl], qkt[2 + tl], b.free], True, True, mark=True)
                    mine.append(t)
                    s = S[2 + n % 2]
                    x = s.ap[:, 0:N]
                    t1 = put("act", lambda e: e.activation(x, o, ACT.Abs), t, s.free)
                    t1 = put("act", lambda e: e.activation(x, x, ACT.Exp, scale=-1.0), t1)
                    t1 = put("act", lambda e: e.activation(x, x, ACT.Ln, bias=1.0), t1)
                    t2 = put("dve", lambda e: e.scalar_tensor_tensor(x, o, 0.0, x, ALU.max, ALU.add), t1)
                    t3 = put("pool", lambda e: e.affine_select(out=x[:, 0:128], in_=x[:, 0:128], compare_op=ALU.is_gt, fill=0.0,
                                                               base=0, pattern=[[1, 128]], channel_multiplier=-1), t2)
                    lo = LO[hq % 2][j]
                    lh, ll = LH[:, lo:lo + N], LL[:, lo:lo + N]
                    t4 = put("dve", lambda e: e.tensor_copy(lh, x), t2, t3, st["lr"][j if j < 3 else 3 + hq % 2])
                    t5 = put("pool", lambda e: e.tensor_tensor(ll, x, F(lh), ALU.subtract), t4, t3, st["lr"][j if j < 3 else 3 + hq % 2])
                    s.free = [t5]
                    lt[n] = [t4, t5]
                    Z[n] = (b, o, N, j)

                def stage_b(n):
                    hq, jr = divmod(n, 4)
                    b, o, N, j = Z.pop(n)
                    for j2 in range(j, 4):
                        n2 = 4 * hq + 3 - j2
                        m = T - 128 * j2
                        dst = b.ap[:, (j2 - j) * 128:(j2 - j) * 128 + m]
                        w_ = TRI if j2 == j else NEG
                        lo = LO[hq % 2][j2]
                        mm(dst, w_, LH[:, lo:lo + m], [lt[n2], ct], False, False, False, True)
                        t = mm(dst, w_, LL[:, lo:lo + m], (), False, False, True, True)
                        if j == 0:
                            st["lr"][j2 if j2 < 3 else 3 + hq % 2] = t
                    t = mm(b.ap[:, 0:128], IDR[:, :], MR, [ct], False, True, True, True)
                    s = S[4 + n % 2]
                    x = s.ap[:, 0:N]
                    t1 = put("act", lambda e: e.activation(x, o, ACT.Exp), t, s.free)
                    b.free = [t1]
                    eh, el = EH[n % 2][:, 0:N], EL[n % 2][:, 0:N]
                    t2 = put("dve", lambda e: e.tensor_copy(eh, x), t1, st["er"][n % 2])
                    t3 = put("dve", lambda e: e.tensor_tensor(el, x, F(eh), ALU.subtract), t2)
                    s.free = [t3]
                    E_[n] = (N, j, [t2, t3])

                def stage_c(n):
                    hq, jr = divmod(n, 4)
                    tl, hh = divmod(hq, 2)
                    N, j, te = E_.pop(n)
                    b = bank[7]
                    assert gtok[quad] is not None or jr < 3
                    vs = VV[:, 2 * par, j, tl * 128:tl * 128 + 128], VV[:, 2 * par + 1, j, tl * 128:tl * 128 + 128]
                    t = mm3(b.ap[:, j * 128:T], vs[0], vs[1], EH[n % 2][:, 0:N], EL[n % 2][:, 0:N],
                            [te, vtok[quad], b.free if jr == 0 else None], jr == 0, jr == 3, mark=True, skip=True)
                    st["er"][n % 2] = [t]
                    if jr == 3:
                        st["pvs"][par] = t
                        r = slice(64 * hh, 64 * hh + 64)
                        g_ = G[2 * par + tl][r, :]
                        t1 = put("dve", lambda e: e.tensor_tensor(g_, b.ap[r, :], g_, ALU.mult), t, gtok[quad])
                        b.free = [t1]
                        kt = 2 * quad + tl
                        rr = split_scaled(g_, OH[r, kt, :], OL[r, kt, :], 1.0, [t1])
                        gfree[par].append(rr)
                        otok[kt] = [otok[kt], rr]

                for n in range(19):
                    if n >= 3:
                        stage_c(n - 3)
                        yield
                    if 2 <= n <= 17:
                        stage_b(n - 2)
                        yield
                    if n < 16:
                        stage_a(n)
                        yield
                st["prev"] = mine

            g2 = []
            put("act", lambda e: e.preload_act_table_set("natural_log_exp_and_others"), mark=False)
            drain(tiles("sg0", bank[0:2], xk, xtok, toks=g2))
            def gate(t, bs, toks):
                ts, t2, r = [None, None], [None, None], []
                gs, tmps = G[2 * (t % 2):2 * (t % 2) + 2], S[0:2]
                for j in range(2):
                    ts[j] = put("dve", lambda e: e.tensor_tensor(gs[j], bs[j].ap[:, :], RB[:, :], ALU.mult), toks[j], rbt["rb"], list(gfree[t % 2]))
                    bs[j].free = [ts[j]]
                yield
                for j in range(2):
                    t2[j] = put("dve", lambda e: e.tensor_scalar(tmps[j].ap, gs[j], -1.0, 80.0, ALU.mult, ALU.min), ts[j], tmps[j].free)
                yield
                for kw in ({}, {"bias": 1.0}, {"scale": -1.0}):
                    f = ACT.Ln if "bias" in kw else ACT.Exp
                    for j in range(2):
                        t2[j] = put("act", lambda e: e.activation(tmps[j].ap, tmps[j].ap, f, **kw), t2[j])
                    yield
                for j in range(2):
                    t3 = put("dve", lambda e: e.tensor_tensor(gs[j], gs[j], tmps[j].ap, ALU.mult), t2[j], ts[j])
                    tmps[j].free = [t3]
                    r.append(t3)
                gtok[t] = r
                yield

            drain(gate(0, bank[0:2], g2))
            for t in range(1, 4):
                side = stream(chain(pause(6), att(t - 1)), 0.42 if t < 3 else 0.56)
                vt = []
                weave(v_chunk(f"sv{t}", bank[0:2], xk, xtok, 4, vt), side)
                vs = 2 * (t % 2)
                vtok[t] = evac_v(bank[0:2], vt, VV[:, vs], VV[:, vs + 1], 4, True, [st["pvs"][t % 2]])
                if t < 3:
                    g2 = []
                    weave(tiles(f"sg{t}", bank[2:4], xk, xtok, toks=g2), side)
                    gg = stream(gate(t, bank[2:4], g2), 0.3)
                else:
                    gg = stream(iter(()), 1)
                tq, tk2 = [], []
                weave(tiles(f"sq{t}", bank[0:2], xk, xtok, toks=tq), gg, side)
                finish(gg)
                weave(tiles(f"sk{t}", bank[2:4], xk, xtok, toks=tk2), side)
                finish(side)
                for j in range(2):
                    qkt[j] = evac_rb(bank[j], tq[j], S[j], QH[:, j, :], QL[:, j, :], 0.125, st["prev"])
                for j in range(2):
                    qkt[2 + j] = evac_rb(bank[2 + j], tk2[j], S[j], KH[:, j, :], KL[:, j, :], 1.0, st["prev"])
            side = stream(chain(pause(4), att(3)), 0.52)
            g2 = []
            weave(tiles("sg3", bank[0:2], xk, xtok, toks=g2), side)
            drain(gate(3, bank[0:2], g2))
            side[1] = 0.75

            def ok(k):
                return OH[:, k, :], OL[:, k, :]

            out_proj("s", ok, otok, None, side, fin=True)

        GOFF = {"g_ffn1": 0, "g_mix": 16, "g_xattn": 32, "g_mem": 48, "g_ffn2": 64}

        for r in range(4):
            plan(("x", r), a["x"][0, r * 128:(r + 1) * 128, :].rearrange("p (k c) -> p k c", c=128), kind="raw")
        seq = list(stages)
        for sname in seq:
            nm, _, l = sname.partition("_")
            if nm in ("ffn1", "ffn2"):
                plan_ffn(sname, a[f"w_{nm}_gu"][int(l)], a[f"w_{nm}_down"][int(l)])
            elif nm == "mix":
                plan_mix(int(l))
                at = len(units) - 4
                if f"x_{l}" in seq:
                    for r in range(2):
                        units.insert(at + r, ((f"mem{l}", r), a["mem"][0, r * 128:(r + 1) * 128, :].rearrange("p (k c) -> p k c", c=128), None, "raw"))
            elif nm == "x":
                plan_x(int(l))
            elif nm == "diff":
                plan_diff()
            else:
                plan_sb()

        tmp = AF[:, 0:256]
        d0 = put("sp", lambda e: e.dma_start(tmp, consts[:, C_ID:C_ID + 256]), sem="c0", by=16)
        pump()
        d1 = put("sp", lambda e: e.dma_start(BLK, consts[:, C_BLK:C_BLK + 2]), sem="c1", by=16)
        k1 = put("act", lambda e: e.activation(IDR[:, :], tmp[:, 0:128], ACT.Copy), d0)
        ga, gb = AF[:, 256:384], AF[:, 384:512]
        gt = []
        zt = put("dve", lambda e: e.memset(AF[:, 256:512], 0.0))
        dn = 0

        def grow(dst, src):
            nonlocal dn
            gt.append(put("pool" if dn % 3 == 1 else "sp", lambda e: e.dma_start(dst, src), zt, sem=f"g{dn}", by=16))
            dn += 1

        for nm in ("g_ffn1", "g_mix", "g_xattn", "g_mem", "g_ffn2"):
            o = GOFF[nm]
            grow(ga[o:o + 16, :], a[nm].rearrange("l (k p) -> (l k) p", p=128))
        grow(ga[80:88, :], a["g_conv_out"].rearrange("l (k p) -> (l k) p", p=128))
        grow(ga[88:96, :], a["g_att_out"].rearrange("l (k p) -> (l k) p", p=128))
        grow(ga[96:104, :], a["g_final"].rearrange("(k p) -> k p", p=128))
        grow(ga[104:112, :], a["a_norm_2"].rearrange("l (k p) -> (l k) p", p=128))
        grow(ga[112:120, :], a["kv_norm_2"].rearrange("(k p) -> k p", p=128))
        grow(ga[120:128, :], a["b_norm_2"].rearrange("l (k p) -> (l k) p", p=128))
        grow(gb[0:24, :], a["w_conv"].rearrange("l k (m p) -> (l k m) p", p=128))
        grow(gb[24:25, :], a["a_subln_2"])
        for c in range(2):
            grow(gb[25:26, c * 64:c * 64 + 64], a["a_q_norm_2"])
            grow(gb[26:27, c * 64:c * 64 + 64], a["a_k_norm_2"])
        for i, nm in enumerate(("a_lq1_2", "a_lk1_2", "a_lq2_2", "a_lk2_2")):
            grow(AF[0:1, 512 + 64 * i:576 + 64 * i], a[nm])
        for l in range(2):
            grow(BF[0:8, l:l + 1], a["b_f"][l].rearrange("(p o) -> p o", o=1))
        us = [get(("x", r)) for r in range(3)]
        xt = []

        def x_rows(i):
            if i == 3:
                us.append(get(("x", 3)))
            row = us[i][0].rearrange("p k c -> p (k c)")
            for hf in range(2):
                b = bank[2 * (i % 2) + hf]
                for j in range(4):
                    k = 4 * hf + j
                    t = pe_transpose(b.ap[:, j * 128:(j + 1) * 128], row[:, k * 128:(k + 1) * 128], ID,
                                     [us[i][1], k1, b.free if j == 0 else None], j == 3)
                dst = X[:, 4 * hf:4 * hf + 4, i * 128:(i + 1) * 128]
                src = b.ap[:, :].rearrange("p (j t) -> p j t", t=128)
                if hf:
                    t2 = put("act", lambda e, dst=dst, src=src: e.activation(dst, src, ACT.Copy), t)
                else:
                    t2 = put("dve", lambda e, dst=dst, src=src: e.tensor_copy(dst, src), t)
                b.free = [t2]
                xt.append(t2)
            raw_done(us[i], [t])
            pump()

        for i in range(3):
            x_rows(i)
        k3 = put("dve", lambda e: e.memset(ONE, 1.0))
        k4 = put("dve", lambda e: e.memset(NH, -0.5))
        pe_transpose(bank[7].ap[:, 0:128], ga, ID, [k1, gt], False)
        t = pe_transpose(bank[7].ap[:, 128:256], gb, ID, (), True)
        t1 = put("dve", lambda e: e.tensor_copy(GA[:, :], bank[7].ap[:, 0:128]), t)
        t2 = put("dve", lambda e: e.tensor_copy(GB[:, :], bank[7].ap[:, 128:160]), t)
        t3 = put("dve", lambda e: e.tensor_scalar(QG, GB[:, 25:26], 0.125, None, ALU.mult), t2)
        t4 = put("dve", lambda e: e.tensor_scalar(SG, GB[:, 24:25], 0.5 * (1.0 - LAMBDA_INIT), None, ALU.mult), t2)
        t5 = put("dve", lambda e: e.tensor_tensor(GG, GA[:, 96:104], GA[:, 104:112], ALU.mult), t1)
        lr = AF[0:1, 512:768]
        u1 = put("dve", lambda e: e.tensor_tensor(AF[0:1, 768:832], lr[:, 0:64], lr[:, 64:128], ALU.mult), gt)
        u2 = put("dve", lambda e: e.tensor_tensor(AF[0:1, 832:896], lr[:, 128:192], lr[:, 192:256], ALU.mult), gt)
        u3 = put("dve", lambda e: e.reduce_sum(LT[0:1, 0:2], AF[0:1, 768:896].rearrange("p (a c) -> p a c", a=2), AX), u1, u2)
        u4 = put("act", lambda e: e.activation(LT[0:1, 2:4], LT[0:1, 0:2], ACT.Exp), u3)
        u5 = put("dve", lambda e: e.tensor_tensor(LT[0:1, 0:1], LT[0:1, 3:4], LT[0:1, 2:3], ALU.subtract), u4, u3)
        u5 = put("dve", lambda e: e.tensor_scalar(LT[0:1, 0:1], LT[0:1, 0:1], -LAMBDA_INIT, None, ALU.add), u5)
        u6 = put("dve", lambda e: e.memset(AF[0:1, 896:1024], 1.0))
        u7 = mm(bank[7].ap[:, 256:257], AF[0:1, 896:1024], LT[0:1, 0:1], [u5, u6, t1, t2])
        lamtok = put("dve", lambda e: e.tensor_copy(LAM, bank[7].ap[:, 256:257]), u7)
        bank[7].free = [lamtok]
        start = [k1, k3, k4, t1, t2, t3, t4, t5, lamtok, d1, gt]
        for e in ("pe", "act", "dve", "pool"):
            q.hold(e, start)

        def gains(i):
            if i >= len(seq):
                return None
            nm, _, l = seq[i].partition("_")
            if nm == "diff":
                return lambda m: GG[:, m:m + 1]
            if nm == "sb":
                return None
            base = {"ffn1": 0, "mix": 16, "x": 32, "ffn2": 64}[nm]
            return gc(base + 8 * int(l))

        x_rows(3)
        state["upto"] = 6
        pump()
        x_post(range(KT), [xt] * KT, gains(0))
        state["upto"] = len(units)

        snap = q.now()
        for i, sname in enumerate(seq):
            nm, _, l = sname.partition("_")
            nxt = gains(i + 1)
            if nm in ("ffn1", "ffn2"):
                ffn(sname, snap, nxt)
            elif nm == "mix":
                ms = mem_prep(int(l), 48 + 8 * int(l)) if f"x_{l}" in seq else iter(())
                mix(int(l), snap, nxt, ms)
            elif nm == "x":
                xattn(int(l), snap, nxt)
            elif nm == "diff":
                diff(snap, nxt)
            else:
                stick(snap)
            snap = q.now()
            rb.free = snap
            pwfree["rcol"] = snap
        if seq[-1] != "sb":
            for m in range(KT):
                xlast[m] = snap
            for p in range(4):
                drain(store(p))
        q.hold("sp", outs)

        sems = {s: ctx.enter_context(nc.semaphore(f"s_{s}")) for s in q.count}
        block = ctx.enter_context(nc.Block())

        @block.tensor
        def _(e):
            q.run("pe", e, sems)

        @block.scalar
        def _(e):
            q.run("act", e, sems)

        @block.vector
        def _(e):
            q.run("dve", e, sems)

        @block.gpsimd
        def _(e):
            q.run("pool", e, sems)

        @block.sync
        def _(e):
            with nc.allow_non_contiguous_dma(reason="eight gate columns and biases"):
                q.run("sp", e, sems)


_INS = ["x", "mem", "g_ffn1", "w_ffn1_gu", "w_ffn1_down", "g_mix", "w_mix_in", "w_conv", "b_f", "g_conv_out", "g_att_out",
        "w_mix_out", "g_xattn", "g_mem", "w_xq", "w_xkv", "w_xo", "g_ffn2", "w_ffn2_gu", "w_ffn2_down", "g_final",
        "a_norm_2", "a_w_in_2", "a_w_out_2", "a_q_norm_2", "a_k_norm_2", "a_lq1_2", "a_lk1_2", "a_lq2_2", "a_lk2_2",
        "a_subln_2", "kv_norm_2", "w_kv_2", "b_norm_2", "b_w_in_2", "b_w_out_2"]


def kernel(**inputs):
    import numpy as _np
    import concourse.bacc as _bacc
    from concourse import mybir as _mybir
    from concourse.bass_utils import run_bass_kernel_spmd as _run

    nc = _bacc.Bacc("TRN2", target_bir_lowering=False, num_devices=1)
    arrays, args = {}, {}
    for name in _INS:
        v = _np.ascontiguousarray(inputs[name])
        arrays[f"in_{name}_dram"] = v
        args[name] = nc.dram_tensor(f"in_{name}_dram", v.shape, _mybir.dt.from_np(v.dtype), kind="ExternalInput").ap()
    c = shape_constants()
    arrays["in_consts_dram"] = c
    cd = nc.dram_tensor("in_consts_dram", c.shape, _mybir.dt.float32, kind="ExternalInput").ap()
    out = nc.dram_tensor("out_0_dram", (1, T, D), _mybir.dt.float32, kind="ExternalOutput").ap()
    program(nc, args, cd, out, STAGES)
    r = _run(nc, [arrays], core_ids=[0])
    return r.results[0]["out_0_dram"]
```
